# Optimizing a Trainium2 kernel written in Bass

```python
import math
import jax, jax.numpy as jnp
from jax import lax
import numpy as np

D_MODEL = 1024
BATCH = 1
SEQ = 4096
DEPTH = 1

MIX_WIDTH = D_MODEL
A_WIDTH = MIX_WIDTH // 2
A_GROUPS = 8
A_GROUP_DIM = A_WIDTH // A_GROUPS
CHUNK = 128
B_HEADS = 8
HEAD_DIM = 64
B_KV_HEADS = 2
B_GROUP = B_HEADS // B_KV_HEADS
B_WIDTH = B_HEADS * HEAD_DIM
KV_WIDTH = B_KV_HEADS * HEAD_DIM
WINDOW = 128
BLOCK = 128
REL_BUCKETS = 32
REL_MAX_DIST = 128
NORM_EPS = 1e-6
IN_WIDTH = 3 * A_WIDTH + 2 * B_WIDTH + 2 * KV_WIDTH

kernel_name = "hybrid_gmlp_swa_sink_sandwich"

def rms_norm(x, g):
    xf = x.astype(jnp.float32)
    y = xf * lax.rsqrt(jnp.mean(xf * xf, axis=-1, keepdims=True) + NORM_EPS)
    return (y * g.astype(jnp.float32)).astype(x.dtype)

def layer_norm(x, g, b):
    xf = x.astype(jnp.float32)
    mu = jnp.mean(xf, axis=-1, keepdims=True)
    xc = xf - mu
    y = xc * lax.rsqrt(jnp.mean(xc * xc, axis=-1, keepdims=True) + NORM_EPS)
    return (y * g.astype(jnp.float32) + b.astype(jnp.float32)).astype(x.dtype)

def t5_bucket(dist):
    max_exact = REL_BUCKETS // 2
    safe = jnp.maximum(dist, 1).astype(jnp.float32)
    large = max_exact + (jnp.log(safe / max_exact) / math.log(REL_MAX_DIST / max_exact)
                         * (REL_BUCKETS - max_exact)).astype(jnp.int32)
    large = jnp.minimum(large, REL_BUCKETS - 1)
    return jnp.where(dist < max_exact, dist, large)

def chunked_spatial_gating(u, v, ln_g, ln_b, w_s, b_s):
    bsz, seq, _ = v.shape
    n_chunks = seq // CHUNK
    vn = layer_norm(v, ln_g, ln_b).reshape(bsz, n_chunks, CHUNK, A_GROUPS, A_GROUP_DIM)
    causal = jnp.tril(jnp.ones((CHUNK, CHUNK), dtype=bool))
    w = jnp.where(causal[None], w_s, jnp.zeros_like(w_s))
    mixed = jnp.einsum('hij,bcjhd->bcihd', w, vn) + b_s.T[None, None, :, :, None]
    return u * mixed.reshape(bsz, seq, A_WIDTH)

def sliding_window_sink_attention(q, k, v, sinks, rel_bias):
    bsz, seq = q.shape[0], q.shape[1]
    nb = seq // BLOCK
    qb = q.reshape(bsz, nb, BLOCK, B_KV_HEADS, B_GROUP, HEAD_DIM)
    pad = jnp.zeros((bsz, BLOCK, B_KV_HEADS, HEAD_DIM), k.dtype)
    kp = jnp.concatenate([pad, k], axis=1).reshape(bsz, nb + 1, BLOCK, B_KV_HEADS, HEAD_DIM)
    vp = jnp.concatenate([pad, v], axis=1).reshape(bsz, nb + 1, BLOCK, B_KV_HEADS, HEAD_DIM)
    kb = jnp.concatenate([kp[:, :-1], kp[:, 1:]], axis=2)
    vb = jnp.concatenate([vp[:, :-1], vp[:, 1:]], axis=2)

    logits = jnp.einsum('bnqkgd,bnskd->bnkgqs', qb, kb).astype(jnp.float32) * (HEAD_DIM ** -0.5)

    q_loc = jnp.arange(BLOCK)[:, None]
    k_loc = jnp.arange(2 * BLOCK)[None, :]
    dist = q_loc + BLOCK - k_loc
    in_window = (dist >= 0) & (dist < WINDOW)
    key_pos = (jnp.arange(nb)[:, None] - 1) * BLOCK + jnp.arange(2 * BLOCK)[None, :]
    mask = in_window[None] & (key_pos >= 0)[:, None, :]

    bias = rel_bias.astype(jnp.float32)[t5_bucket(jnp.maximum(dist, 0))]
    bias = bias.transpose(2, 0, 1).reshape(B_KV_HEADS, B_GROUP, BLOCK, 2 * BLOCK)
    logits = jnp.where(mask[None, :, None, None], logits + bias, jnp.float32(-1e30))

    sink = sinks.astype(jnp.float32).reshape(B_KV_HEADS, B_GROUP)[None, None, :, :, None, None]
    m = jnp.maximum(jnp.max(logits, axis=-1, keepdims=True), sink)
    e = jnp.exp(logits - m)
    probs = e / (jnp.sum(e, axis=-1, keepdims=True) + jnp.exp(sink - m))
    out = jnp.einsum('bnkgqs,bnskd->bnqkgd', probs.astype(vb.dtype), vb)
    return out.reshape(bsz, seq, B_WIDTH)

def hybrid_layer(x, pre_g, w_in, ln_g, ln_b, w_s, b_s, sinks, rel_bias, w_out, post_g):
    bsz, seq, _ = x.shape
    h = rms_norm(x, pre_g)
    proj = h @ w_in
    splits = [2 * A_WIDTH, 3 * A_WIDTH, 3 * A_WIDTH + B_WIDTH,
              3 * A_WIDTH + B_WIDTH + KV_WIDTH, 3 * A_WIDTH + B_WIDTH + 2 * KV_WIDTH]
    a_uv, a_z, q, k, v, b_z = jnp.split(proj, splits, axis=-1)

    a_uv = jax.nn.gelu(a_uv)
    u, vv = jnp.split(a_uv, 2, axis=-1)
    y_a = chunked_spatial_gating(u, vv, ln_g, ln_b, w_s, b_s) * jax.nn.silu(a_z)

    q = q.reshape(bsz, seq, B_HEADS, HEAD_DIM)
    k = k.reshape(bsz, seq, B_KV_HEADS, HEAD_DIM)
    v = v.reshape(bsz, seq, B_KV_HEADS, HEAD_DIM)
    y_b = sliding_window_sink_attention(q, k, v, sinks, rel_bias) * jax.nn.silu(b_z)

    y = jnp.concatenate([y_a, y_b], axis=-1) @ w_out
    return x + rms_norm(y, post_g)

def setup_inputs(seed: int = 0) -> dict:
    key = jax.random.key(seed)
    ks = jax.random.split(key, 12)
    f32 = jnp.float32
    x = jax.random.normal(ks[0], (BATCH, SEQ, D_MODEL), f32)
    pre_norm_g = 1.0 + 0.05 * jax.random.normal(ks[1], (DEPTH, D_MODEL), f32)
    w_in = jax.random.normal(ks[2], (DEPTH, D_MODEL, IN_WIDTH), f32) * (D_MODEL ** -0.5)
    ln_v_g = 1.0 + 0.05 * jax.random.normal(ks[3], (DEPTH, A_WIDTH), f32)
    ln_v_b = 0.02 * jax.random.normal(ks[4], (DEPTH, A_WIDTH), f32)
    w_spatial = jax.random.normal(ks[5], (DEPTH, A_GROUPS, CHUNK, CHUNK), f32) * (CHUNK ** -0.5)
    b_spatial = 1.0 + 0.1 * jax.random.normal(ks[6], (DEPTH, A_GROUPS, CHUNK), f32)
    sinks = 0.5 * jax.random.normal(ks[7], (DEPTH, B_HEADS), f32)
    rel_bias = 0.5 * jax.random.normal(ks[8], (REL_BUCKETS, B_HEADS), f32)
    w_out = jax.random.normal(ks[9], (DEPTH, MIX_WIDTH, D_MODEL), f32) * (MIX_WIDTH ** -0.5)
    post_norm_g = 1.0 + 0.05 * jax.random.normal(ks[10], (DEPTH, D_MODEL), f32)
    return {"x": x, "pre_norm_g": pre_norm_g, "w_in": w_in, "ln_v_g": ln_v_g, "ln_v_b": ln_v_b,
            "w_spatial": w_spatial, "b_spatial": b_spatial, "sinks": sinks, "rel_bias": rel_bias,
            "w_out": w_out, "post_norm_g": post_norm_g}

def reference(x, pre_norm_g, w_in, ln_v_g, ln_v_b, w_spatial, b_spatial, sinks, rel_bias,
              w_out, post_norm_g):
    for layer in range(DEPTH):
        x = hybrid_layer(x, pre_norm_g[layer], w_in[layer], ln_v_g[layer], ln_v_b[layer],
                         w_spatial[layer], b_spatial[layer], sinks[layer], rel_bias,
                         w_out[layer], post_norm_g[layer])
    return x


_drawn_inputs = setup_inputs


def setup_inputs(seed=0):
    import zlib

    import numpy as np

    out = dict(_drawn_inputs(seed))
    spreads = {}
    factors = {'ln_v_g': 3.188, 'ln_v_b': 7.697, 'sinks': 64.0}
    for name, (base, spread) in spreads.items():
        noise = np.random.default_rng([zlib.crc32(name.encode()), seed]).standard_normal(out[name].shape)
        drawn = base * np.exp(spread * noise) if base else spread * noise
        out[name] = __import__('jax').numpy.asarray(drawn.astype(out[name].dtype))
    for name, factor in factors.items():
        out[name] = (out[name] * factor).astype(out[name].dtype)
    return out
```

```python
from contextlib import ExitStack
import math

import numpy as np
import concourse.bass as bass
from concourse import mybir

F32 = mybir.dt.float32
F32R = mybir.dt.float32r
I32 = mybir.dt.int32
ALU = mybir.AluOpType
ACTF = mybir.ActivationFunctionType

P = 128
MASKED = -1e30
NORM_EPS = 1e-6
REL_MAX_DIST = 128
STATS = 6
HALF = 512
RSQRT_STEPS = 10
X_SLOTS = 3


def ge(eng, sem, value):
    if isinstance(value, int) and value <= 0:
        return
    eng.wait_ge(sem, value)


def rsqrt(dve, sem, base, x, y, tmp):
    done = 0

    def link(ins):
        nonlocal done
        done += 1
        ins.then_inc(sem, 1)
        dve.wait_ge(sem, base + done)

    link(dve.tensor_scalar(y.bitcast(I32), x.bitcast(I32), -0.5, 1597463007.0, ALU.mult, ALU.add))
    for _ in range(3):
        link(dve.scalar_tensor_tensor(out=tmp, in0=y, scalar=y, in1=x, op0=ALU.mult, op1=ALU.mult))
        link(dve.tensor_scalar(tmp, tmp, -0.5, 1.5, ALU.mult, ALU.add))
        link(dve.tensor_tensor(y, y, tmp, ALU.mult))
    assert done == RSQRT_STEPS


def build(nc, x, pre_g, w_in, ln_g, ln_b, w_spatial, b_spatial, sinks, rel_bias, w_out, post_g,
          bucket_onehot, identity, out):
    _, SEQ, D = x.shape
    AW = ln_g.shape[1]
    AG = w_spatial.shape[1]
    AD = AW // AG
    H = sinks.shape[1]
    BUCKETS = rel_bias.shape[0]
    HD = (w_out.shape[1] - AW) // H
    BW = H * HD
    KVW = (w_in.shape[2] - 3 * AW - 2 * BW) // 2
    G = KVW // HD
    GH = H // G
    NB = SEQ // P
    KT = D // P
    BCOLS = 2 * BW + 2 * KVW
    ACOLS = 3 * AW
    assert D == 2 * HALF and AW == HALF and BW == HALF and HD == 64 and H == 8 and G == 2 and NB == 32

    y_scratch = nc.dram_tensor("y_b_scratch", [NB, P, BW], F32, kind="Internal").ap()
    PITCH = 3 * P
    bias_scratch = nc.dram_tensor("bias_scratch", [H, P, PITCH], F32, kind="Internal")

    x_blocks = x.rearrange("o (n p) d -> (o n) p d", p=P)
    out_blocks = out.rearrange("o (n p) d -> (o n) p d", p=P)

    ctx = ExitStack()
    with ctx:
        def sb(stack, name, shape, dt=F32):
            return stack.enter_context(nc.sbuf_tensor(name, shape, dt))

        ident = sb(ctx, "ident", [P, P])
        post_gain = sb(ctx, "post_gain", [P, D])
        ln_gain = sb(ctx, "ln_gain", [P, AW])
        ln_bias = sb(ctx, "ln_bias", [P, AW])
        ws_t = sb(ctx, "ws_t", [P, AG, P])
        bs_t = sb(ctx, "bs_t", [P, AG])
        gain = sb(ctx, "gain", [P, KT])
        neg_sink = sb(ctx, "neg_sink", [P, H])
        rstd_all = sb(ctx, "rstd_all", [P, NB])
        small = sb(ctx, "small", [P, 32])
        stats = sb(ctx, "stats", [P, 2, STATS])
        xs = sb(ctx, "xs", [P, X_SLOTS, D])
        act_buf = sb(ctx, "act_buf", [P, 3, HALF])
        xt = sb(ctx, "xt", [P, 2, 2, KT, P], F32R)

        weights_b = ExitStack()
        wb_hi = sb(weights_b, "wb_hi", [P, KT, BCOLS], F32R)
        wb_lo = sb(weights_b, "wb_lo", [P, KT, BCOLS], F32R)
        stage_c = sb(weights_b, "stage_c", [P, 2, ACOLS])
        weights_b.close()
        wa_hi = sb(ctx, "wa_hi", [P, KT, ACOLS], F32R)
        wa_lo = sb(ctx, "wa_lo", [P, KT, ACOLS], F32R)

        work = ExitStack()
        start = ExitStack()
        bias = sb(work, "bias", [P, H, 3 * P])
        stage_b = sb(start, "stage_b", [P, KT, BCOLS])
        bias_rows = sb(start, "bias_rows", [P, H, PITCH])
        start.close()
        stage_a = sb(work, "stage_a", [P, 2, ACOLS])
        q_tok = sb(work, "q_tok", [P, H, 2, HD])
        k_tok = sb(work, "k_tok", [P, 2, G, 2, HD])
        v_tok = sb(work, "v_tok", [P, 2, KVW])
        gate_b = sb(work, "gate_b", [P, 2, BW])
        q_stack = sb(work, "q_stack", [P, H, P], F32R)
        k_stack = sb(work, "k_stack", [P, 2 * G, 2, P], F32R)
        probs = sb(work, "probs", [P, H, 2 * P])
        probs_t = sb(work, "probs_t", [P, H, 2, P])
        y_b = sb(work, "y_b", [P, 2, BW])
        row = sb(work, "row", [P, 6, H])
        work.close()
        wo_hi = sb(ctx, "wo_hi", [P, KT, D], F32R)
        wo_lo = sb(ctx, "wo_lo", [P, KT, D], F32R)

        row_max, neg_max, sink_diff, row_sum, sink_exp, row_inv = (row[:, j, :] for j in range(6))
        mean_var = small[:, 0:2]
        mean_sq, newton = small[:, 2:3], small[:, 3:4]
        rstd_ln, rstd_post = small[:, 4:5], small[:, 5:6]

        def rstd_b(slot, j):
            return small[:, 8 + 3 * slot + j:9 + 3 * slot + j]

        def rstd_a(slot, j):
            return small[:, 16 + 2 * slot + j:17 + 2 * slot + j]

        v_act, gate_a, yb_in = (act_buf[:, j, :] for j in range(3))
        xt_a, yt_a = xt[:, 0], xt[:, 1]
        onehot = xs[0:BUCKETS, 2, 0:P]
        rel = xs[0:BUCKETS, 2, P:P + H]
        ones = xs[0:BUCKETS, 2, 2 * P:3 * P]
        rel_rows = act_buf[0:BUCKETS, 0:2, :].rearrange("p a b -> p (a b)").rearrange("p (h j) -> p h j", h=H)
        wo_stage = (xs[:, 2, :], act_buf[:, 0:2, :].rearrange("p a b -> p (a b)"))

        bank = [ctx.enter_context(nc.psum_tensor(f"bank{j}", [P, HALF], F32)) for j in range(8)]
        Q_BANK, KV_BANK, Z_BANK, T_BANK, O_BANK = 0, 1, 2, 3, 7

        def sem(name):
            return ctx.enter_context(nc.semaphore(name))

        ident_in, gain_in, consts_in, ws_in, buckets_in, bias_out, bias_in = (sem(s) for s in (
            "ident_in", "gain_in", "consts_in", "ws_in", "buckets_in", "bias_out", "bias_in"))
        ones_set, rel_spread, rel_summed, rows_set, sink_negated = (sem(s) for s in (
            "ones_set", "rel_spread", "rel_summed", "rows_set", "sink_negated"))
        ws_masked = sem("ws_masked")
        wb_in = [sem(f"wb_in{k}") for k in range(KT)]
        wa_in = [sem(f"wa_in{j}") for j in range(4)]
        wo_in = [sem(f"wo_in{j}") for j in range(2)]
        wb_hi_set, wb_lo_set, wa_hi_set, wa_lo_set, wo_hi_set, wo_lo_set = (sem(s) for s in (
            "wb_hi_set", "wb_lo_set", "wa_hi_set", "wa_lo_set", "wo_hi_set", "wo_lo_set"))
        x_in = [sem(f"x_in{j}") for j in range(2)]
        x_turned, xt_hi_set, xt_lo_set, x_read, rstd_set = (sem(s) for s in (
            "x_turned", "xt_hi_set", "xt_lo_set", "x_read", "rstd_set"))
        projected, q_hi_set, k_hi_set, v_set, z_tanh_set, q_lo_set, k_lo_set, gate_b_set = (sem(s) for s in (
            "projected", "q_hi_set", "k_hi_set", "v_set", "z_tanh_set", "q_lo_set", "k_lo_set", "gate_b_set"))
        qk_turned, stacked, scored, max_set, exp_set, sink_exp_set = (sem(s) for s in (
            "qk_turned", "stacked", "scored", "max_set", "exp_set", "sink_exp_set"))
        p_turned, p_copied_act, p_copied_dve, attended, o_read, yb_set = (sem(s) for s in (
            "p_turned", "p_copied_act", "p_copied_dve", "attended", "o_read", "yb_set"))
        yb_stored = [sem(f"yb_stored{j}") for j in range(2)]
        stats_steps, softmax_steps, gate_steps, denominator_steps = (sem(s) for s in (
            "stats_steps", "softmax_steps", "gate_steps", "denominator_steps"))
        xa_in = [sem(f"xa_in{j}") for j in range(X_SLOTS)]
        yb_loaded = sem("yb_loaded")
        xa_turned, xa_hi_set, xa_lo_set, rstd_a_set = (sem(s) for s in (
            "xa_turned", "xa_hi_set", "xa_lo_set", "rstd_a_set"))
        a_projected, v_act_set, za_tanh_set, u_act_set, z_read, u_read, vn_set = (sem(s) for s in (
            "a_projected", "v_act_set", "za_tanh_set", "u_act_set", "z_read", "u_read", "vn_set"))
        mixed, ya_set, y_turned, yt_hi_set, yt_lo_set, y_projected, post_set = (sem(s) for s in (
            "mixed", "ya_set", "y_turned", "yt_hi_set", "yt_lo_set", "y_projected", "post_set"))
        out_stored = [sem(f"out_stored{j}") for j in range(X_SLOTS)]
        ln_steps, gate_a_steps, post_steps, rstd_a_steps, ya_steps = (sem(s) for s in (
            "ln_steps", "gate_a_steps", "post_steps", "rstd_a_steps", "ya_steps"))

        def later(p, b, d):
            return p + (b + d) // 2, (b + d) % 2

        def index(p, b):
            return 2 * p + b

        def exists(p, b):
            n = index(p, b)
            return not isinstance(n, int) or 0 <= n < NB

        def run_b(eng, step):
            for s in range(3):
                step(s // 2, s % 2)
            with eng.Fori(0, (NB - 4) // 2) as i:
                step(i + 1, 1)
                step(i + 2, 0)
            for s in range(NB - 1, NB + 2):
                step(s // 2, s % 2)

        def later_a(p, b, d):
            return p + (b + d) // 3, (b + d) % 3

        def index_a(p, b):
            return 3 * p + b

        def exists_a(p, b):
            n = index_a(p, b)
            return not isinstance(n, int) or 0 <= n < NB

        def run_a(eng, step):
            step(0, 0)
            with eng.Fori(0, (NB - 2) // 3) as i:
                step(i, 1)
                step(i, 2)
                step(i + 1, 0)
            for s in range(NB - 1, NB + 1):
                step(s // 3, s % 3)

        def row_of(blocks, n):
            if isinstance(n, int):
                return blocks[n]
            return blocks[bass.ds(n, 1)].rearrange("n p d -> p (n d)")

        block = ctx.enter_context(nc.Block())

        @block.sync
        def _(sp):
            sp.dma_start(ident[:, :], identity).then_inc(ident_in, 16)
            sp.dma_start(xs[:, 0, :], x_blocks[0]).then_inc(x_in[0], 16)
            sp.dma_start(gain[:, :], pre_g).then_inc(gain_in, 16)
            w_rows = w_in[0].rearrange("(k p) c -> k p c", p=P)
            wo_rows = w_out[0].rearrange("(k p) c -> k p c", p=P)
            for k in range(KT):
                sp.dma_start(stage_b[:, k, :], w_rows[k, :, ACOLS:]).then_inc(wb_in[k], 16)
                if k == 0:
                    sp.dma_start(xs[:, 1, :], x_blocks[1]).then_inc(x_in[1], 16)
            sp.wait_ge(rows_set, 2)
            sp.dma_start(bias_scratch.ap().rearrange("h p j -> p h j"), bias_rows[:, :, :]).then_inc(bias_out, 16)
            sp.wait_ge(bias_out, 16)
            for at, keys in ((0, 2 * P), (2 * P, P)):
                sp.dma_start(bias[:, :, at:at + keys],
                             bass.AP(bias_scratch, P - 1, [[PITCH - 1, P], [P * PITCH, H], [1, keys]])).then_inc(bias_in, 16)

            def step(p, b):
                pp, slot = later(p, b, 1)
                if exists(pp, slot) and exists(*later(p, b, -1)):
                    n = index(p, b)
                    sp.wait_ge(x_turned, 2 * n)
                    sp.wait_ge(x_read, n)
                    sp.dma_start(xs[:, slot, :], row_of(x_blocks, n + 1)).then_inc(x_in[slot], 16)
                if exists(*later(p, b, -2)):
                    n = index(p, b) - 2
                    sp.wait_ge(yb_set, n + 1)
                    sp.dma_start(row_of(y_scratch, n), y_b[:, b, :]).then_inc(yb_stored[b], 16)

            run_b_done = []

            def step_b(p, b):
                s = index(p, b)
                if isinstance(s, int) and s == NB - 1:
                    for k in range(4):
                        sp.dma_start((stage_a if k < 2 else stage_c)[:, k % 2, :],
                                     w_rows[k, :, 0:ACOLS]).then_inc(wa_in[k], 16)
                step(p, b)
                run_b_done.append(s)

            run_b(sp, step_b)
            sp.wait_ge(x_turned, 2 * NB)
            sp.wait_ge(x_read, NB)
            for j in range(2):
                sp.dma_start(xs[:, j, :], x_blocks[j]).then_inc(xa_in[j], 16)
            for k in range(4, KT):
                sp.wait_ge(wa_lo_set, k - 3 if k < 6 else k - 1)
                sp.dma_start(stage_a[:, k % 2, :], w_rows[k, :, 0:ACOLS]).then_inc(wa_in[k % 2], 16)
            for k in range(KT):
                if k >= 2:
                    sp.wait_ge(wo_lo_set, k - 1)
                sp.dma_start(wo_stage[k % 2], wo_rows[k]).then_inc(wo_in[k % 2], 16)
            for j in range(2):
                sp.wait_ge(yb_stored[j], 16 * (NB // 2))
            sp.wait_ge(wo_lo_set, KT)

            def step_a(p, b):
                n = index_a(p, b)
                if exists_a(*later_a(p, b, 1)) and not (isinstance(n, int) and n == 0):
                    before, slot = later_a(p, b, -2)
                    if exists_a(before, slot):
                        sp.wait_ge(out_stored[slot], 16 * before + 16)
                    sp.dma_start(xs[:, slot, :], row_of(x_blocks, n + 1)).then_inc(xa_in[slot], 16)
                if exists_a(p, b):
                    ge(sp, y_turned, 2 * n)
                    sp.dma_start(yb_in, row_of(y_scratch, n)).then_inc(yb_loaded, 16)
                if exists_a(*later_a(p, b, -1)):
                    _, slot = later_a(p, b, -1)
                    sp.wait_ge(post_set, n)
                    sp.dma_start(row_of(out_blocks, n - 1), xs[:, slot, :]).then_inc(out_stored[slot], 16)

            run_a(sp, step_a)
            for j in range(X_SLOTS):
                sp.wait_ge(out_stored[j], 16 * len(range(j, NB, X_SLOTS)))

        @block.gpsimd
        def _(pool):
            for target, source in ((post_gain, post_g[0]), (ln_gain, ln_g[0]), (ln_bias, ln_b[0]), (neg_sink, sinks[0])):
                pool.dma_start(target[:, :], source.partition_broadcast(P)).then_inc(consts_in, 16)
            pool.dma_start(bs_t[:, :], b_spatial).then_inc(consts_in, 16)
            pool.dma_start(onehot, bucket_onehot).then_inc(buckets_in, 16)
            pool.dma_start(rel, rel_bias).then_inc(buckets_in, 16)
            pool.dma_start(ws_t[:, :, :], w_spatial).then_inc(ws_in, 16)
            pool.memset(ones, 1.0).then_inc(ones_set, 1)
            pool.wait_ge(ws_in, 16)
            pool.affine_select(out=ws_t[:, :, :], in_=ws_t[:, :, :], compare_op=ALU.is_ge, fill=0.0, base=0,
                               pattern=[[0, AG], [1, P]], channel_multiplier=-1).then_inc(ws_masked, 1)

        @block.tensor
        def _(pe):
            def turn(target, source):
                return pe.transpose(target, source, ident[:, :])

            def turn_x(p, b):
                n = index(p, b)
                pe.wait_ge(x_in[b], 16 * p + 16)
                ge(pe, xt_lo_set, 2 * n)
                ge(pe, p_copied_act, 2 * (n - 3) + 1 if not isinstance(n, int) or n >= 3 else 0)
                ge(pe, p_copied_dve, 2 * (n - 3) + 1 if not isinstance(n, int) or n >= 3 else 0)
                for half in range(2):
                    for k in range(4):
                        last = turn(bank[T_BANK + half][:, k * P:(k + 1) * P],
                                    xs[:, b, (4 * half + k) * P:(4 * half + k + 1) * P])
                    last.then_inc(x_turned, 1)

            def project_k(p, b, k):
                n = index(p, b)
                if k == 0:
                    pe.wait_ge(xt_lo_set, 2 * n + 2)
                if isinstance(n, int) and n == 0:
                    pe.wait_ge(wb_lo_set, k + 1)
                cols = ((Q_BANK, 0, BW, q_lo_set), (KV_BANK, BW, BW + 2 * KVW, k_lo_set),
                        (Z_BANK, BW + 2 * KVW, BCOLS, gate_b_set))
                for part in range(2):
                    for j, a, e, emptied in cols:
                        if k == 0 and part == 0:
                            ge(pe, emptied, n)
                        for w in (wb_hi, wb_lo)[:2 - part]:
                            last = pe.matmul(bank[j][:, 0:e - a], xt[:, b, part, k, :], w[:, k, a:e],
                                             start=(k == 0 and part == 0 and w is wb_hi),
                                             stop=(k == KT - 1 and part == 1))
                if k == KT - 1:
                    last.then_inc(projected, 1)

            def turn_qk(p, b, s):
                n = index(p, b)
                pe.wait_ge(q_lo_set, n + 1)
                pe.wait_ge(k_lo_set, n + 1)
                if exists(*later(p, b, 2)):
                    pe.wait_ge(xt_lo_set, 2 * (n + 2) + 2)
                for h in range(H):
                    last = turn(bank[T_BANK + h // 4][:, (h % 4) * P:(h % 4 + 1) * P],
                                q_tok[:, h, :, :].rearrange("p a d -> p (a d)"))
                    if h % 4 == 3:
                        last.then_inc(qk_turned, 1)
                ge(pe, p_copied_act, 2 * n)
                for j in range(2 * G):
                    last = turn(bank[T_BANK + 2][:, j * P:(j + 1) * P],
                                k_tok[:, j // G, j % G, :, :].rearrange("p a d -> p (a d)"))
                last.then_inc(qk_turned, 1)

            def first_block(p, b):
                n = index(p, b)
                return isinstance(n, int) and n == 0

            def score(p, b):
                n = index(p, b)
                keys = P if first_block(p, b) else 2 * P
                pe.wait_ge(stacked, 3 * n + 3)
                ge(pe, p_copied_dve, 2 * n)
                for h in range(H):
                    for part in range(2):
                        moving = k_stack[:, part * G + h // GH, :, :].rearrange("p s k -> p (s k)")
                        last = pe.matmul(bank[T_BANK + h // 2][:, (h % 2) * 2 * P:(h % 2) * 2 * P + keys],
                                         q_stack[:, h, :], moving[:, 0:keys],
                                         start=(part == 0), stop=(part == 1))
                    if h % 2 == 1:
                        last.then_inc(scored, 1)

            def turn_probs(p, b, half):
                n = index(p, b)
                for h in range(4 * half, 4 * half + 4):
                    pe.wait_ge(exp_set, 8 * n + h + 1)
                    for s in range(1 if first_block(p, b) else 2):
                        at = ((h % 2) * 2 + s) * P
                        last = turn(bank[T_BANK + h // 2][:, at:at + P], probs[:, h, s * P:(s + 1) * P])
                    if h % 2 == 1:
                        last.then_inc(p_turned, 1)

            def attend(p, b):
                n = index(p, b)
                pe.wait_ge(p_copied_act, 2 * n + 2)
                pe.wait_ge(p_copied_dve, 2 * n + 2)
                pe.wait_ge(v_set, n + 1)
                ge(pe, o_read, n)
                slots = range(1 if first_block(p, b) else 2)
                for h in range(H):
                    g = h // GH
                    for s in slots:
                        last = pe.matmul(bank[O_BANK][:, h * HD:(h + 1) * HD], probs_t[:, h, s, :],
                                         v_tok[:, s, g * HD:(g + 1) * HD],
                                         start=(s == 0), stop=(s == slots[-1]))
                last.then_inc(attended, 1)

            def step(p, b):
                s = index(p, b)
                now, ahead, behind, last = (p, b), later(p, b, 1), later(p, b, -1), later(p, b, -2)
                if exists(*ahead):
                    turn_x(*ahead)
                if exists(*last):
                    attend(*last)
                for k in range(KT):
                    if exists(*now):
                        project_k(*now, k)
                    if exists(*behind):
                        if k == 1:
                            turn_qk(*behind, s)
                        if k == 3:
                            score(*behind)
                        if k == 6:
                            turn_probs(*behind, 0)
                        if k == 7:
                            turn_probs(*behind, 1)

            pe.wait_ge(ident_in, 16)
            turn_x(0, 0)
            pe.wait_ge(ones_set, 1)
            pe.wait_ge(rel_spread, H)
            for half in range(2):
                pe.matmul(bank[5 + half][:, :], ones, rel_rows[:, 4 * half:4 * half + 4, :].rearrange("b h j -> b (h j)"),
                          start=True, stop=True).then_inc(rel_summed, 1)
            pe.wait_ge(rows_set, 2)
            run_b(pe, step)

            def turn_xa(p, b):
                n = index_a(p, b)
                pe.wait_ge(xa_in[b], 16 * p + 16)
                ge(pe, yt_lo_set, 2 * (n - 1))
                for half in range(2):
                    for k in range(4):
                        last = turn(bank[5 + half][:, k * P:(k + 1) * P],
                                    xs[:, b, (4 * half + k) * P:(4 * half + k + 1) * P])
                    last.then_inc(xa_turned, 1)

            def project_a(p, b, k):
                n = index_a(p, b)
                if k == 0:
                    pe.wait_ge(xa_lo_set, 2 * n + 2)
                if isinstance(n, int) and n == 0:
                    pe.wait_ge(wa_lo_set, k + 1)
                for part in range(2):
                    for j, emptied in ((1, v_act_set), (2, z_read), (0, u_read)):
                        if k == 0 and part == 0:
                            ge(pe, emptied, n)
                        for w in (wa_hi, wa_lo)[:2 - part]:
                            last = pe.matmul(bank[j][:, :], xt_a[:, part, k, :], w[:, k, j * AW:(j + 1) * AW],
                                             start=(k == 0 and part == 0 and w is wa_hi),
                                             stop=(k == KT - 1 and part == 1))
                if k == KT - 1:
                    last.then_inc(a_projected, 1)

            def turn_y(p, b):
                n = index_a(p, b)
                if exists_a(*later_a(p, b, 1)):
                    pe.wait_ge(xa_lo_set, 2 * (n + 1) + 2)
                pe.wait_ge(ya_set, n + 1)
                for k in range(4):
                    last = turn(bank[5][:, k * P:(k + 1) * P], gate_a[:, k * P:(k + 1) * P])
                last.then_inc(y_turned, 1)
                pe.wait_ge(yb_loaded, 16 * n + 16)
                for k in range(4):
                    last = turn(bank[6][:, k * P:(k + 1) * P], yb_in[:, k * P:(k + 1) * P])
                last.then_inc(y_turned, 1)

            def project_y(p, b, k):
                n = index_a(p, b)
                if k % 4 == 0:
                    pe.wait_ge(yt_lo_set, 2 * n + 1 + k // 4)
                if k == 0:
                    ge(pe, post_set, n)
                if isinstance(n, int) and n == 0:
                    pe.wait_ge(wo_lo_set, k + 1)
                for part in range(2):
                    for half in range(2):
                        for w in (wo_hi, wo_lo)[:2 - part]:
                            last = pe.matmul(bank[3 + half][:, :], yt_a[:, part, k, :],
                                             w[:, k, half * HALF:(half + 1) * HALF],
                                             start=(k == 0 and part == 0 and w is wo_hi),
                                             stop=(k == KT - 1 and part == 1))
                if k == KT - 1:
                    last.then_inc(y_projected, 1)

            def mix(p, b):
                n = index_a(p, b)
                pe.wait_ge(vn_set, n + 1)
                for g in range(AG):
                    last = pe.matmul(bank[O_BANK][:, g * AD:(g + 1) * AD], ws_t[:, g, :],
                                     v_act[:, g * AD:(g + 1) * AD], start=True, stop=True)
                last.then_inc(mixed, 1)

            def step_a(p, b):
                now, ahead, behind = (p, b), later_a(p, b, 1), later_a(p, b, -1)
                for k in range(KT):
                    if exists_a(*now):
                        project_a(*now, k)
                    if k == 1 and exists_a(*behind):
                        turn_y(*behind)
                for k in range(KT):
                    if exists_a(*behind):
                        project_y(*behind, k)
                    if k == 1 and exists_a(*ahead):
                        turn_xa(*ahead)
                    if k == 4 and exists_a(*now):
                        mix(*now)

            pe.wait_ge(ws_masked, 1)
            pe.wait_ge(p_copied_act, 2 * NB)
            pe.wait_ge(p_copied_dve, 2 * NB)
            pe.wait_ge(o_read, NB)
            turn_xa(0, 0)
            run_a(pe, step_a)

        @block.scalar
        def _(act):
            def copy(target, source, scale=1.0):
                return act.activation(target, source, ACTF.Copy, scale=scale)

            def turned_hi(p, b):
                n = index(p, b)
                for half in range(2):
                    act.wait_ge(x_turned, 2 * n + 1 + half)
                    copy(xt[:, b, 0, 4 * half:4 * half + 4, :], bank[T_BANK + half][:, :]
                         .rearrange("p (k t) -> p k t", k=4)).then_inc(xt_hi_set, 1)

            def leave_projection(p, b):
                n = index(p, b)
                act.wait_ge(rstd_set, n + 1)
                act.wait_ge(projected, n + 1)
                copy(q_tok[:, :, 0, :].bitcast(F32R), bank[Q_BANK][:, :].rearrange("p (h d) -> p h d", h=H),
                     rstd_b(b, 1)).then_inc(q_hi_set, 1)
                for c in range(2):
                    last = copy(k_tok[:, 0, :, c, :].bitcast(F32R),
                                bank[KV_BANK][:, 0:KVW].rearrange("p (g d) -> p g d", g=G), rstd_b(b, 0))
                last.then_inc(k_hi_set, 1)
                ge(act, yb_set, n - 1)
                act.activation(gate_b[:, b, :], bank[Z_BANK][:, :], ACTF.Tanh, scale=rstd_b(b, 2)).then_inc(z_tanh_set, 1)
                ge(act, attended, n)
                copy(v_tok[:, b, :], bank[KV_BANK][:, KVW:2 * KVW], rstd_b(b, 0)).then_inc(v_set, 1)

            def stack(p, b):
                n = index(p, b)
                for j in range(2):
                    act.wait_ge(qk_turned, 3 * n + 1 + j)
                    copy(q_stack[:, 4 * j:4 * j + 4, :], bank[T_BANK + j][:, :]
                         .rearrange("p (h t) -> p h t", h=4)).then_inc(stacked, 1)
                act.wait_ge(qk_turned, 3 * n + 3)
                copy(k_stack[:, :, b, :], bank[T_BANK + 2][:, :].rearrange("p (j t) -> p j t", j=2 * G)).then_inc(stacked, 1)

            def exponentials(p, b):
                n = index(p, b)
                keys = P if isinstance(n, int) and n == 0 else 2 * P
                for h in range(H):
                    if h % 4 == 0:
                        act.wait_ge(max_set, 2 * n + 1 + h // 4)
                    act.activation(probs[:, h, 0:keys], probs[:, h, 0:keys], ACTF.Exp,
                                   bias=neg_max[:, h:h + 1], accum_out=row_sum[:, h:h + 1]).then_inc(exp_set, 1)
                act.activation(sink_exp, sink_diff, ACTF.Exp).then_inc(sink_exp_set, 1)

            def leave_probs(p, b):
                n = index(p, b)
                used = 1 if isinstance(n, int) and n == 0 else 2
                for j in (0, 2):
                    act.wait_ge(p_turned, 4 * n + 1 + j)
                    copy(probs_t[:, 2 * j:2 * j + 2, 0:used, :],
                         bank[T_BANK + j][:, :].rearrange("p (h s t) -> p h s t", h=2, s=2)[:, :, 0:used, :]).then_inc(p_copied_act, 1)

            def step(p, b):
                ahead, behind = later(p, b, 1), later(p, b, -1)
                if exists(*behind):
                    leave_projection(*behind)
                if exists(*ahead):
                    turned_hi(*ahead)
                if exists(*behind):
                    stack(*behind)
                    exponentials(*behind)
                    leave_probs(*behind)

            turned_hi(0, 0)
            act.wait_ge(gain_in, 16)
            for k in range(KT):
                act.wait_ge(wb_in[k], 16)
                copy(wb_hi[:, k, :], stage_b[:, k, :], gain[:, k:k + 1]).then_inc(wb_hi_set, 1)
            run_b(act, step)

            def turned_hi_a(p, b):
                n = index_a(p, b)
                for half in range(2):
                    act.wait_ge(xa_turned, 2 * n + 1 + half)
                    copy(xt_a[:, 0, 4 * half:4 * half + 4, :],
                         bank[5 + half][:, :].rearrange("p (k t) -> p k t", k=4)).then_inc(xa_hi_set, 1)

            def leave_projection_a(p, b):
                n = index_a(p, b)
                act.wait_ge(rstd_a_set, n + 1)
                act.wait_ge(a_projected, n + 1)
                ge(act, post_set, n - 1)
                act.activation(v_act, bank[1][:, :], ACTF.Gelu_apprx_tanh, scale=rstd_a(b, 0)).then_inc(v_act_set, 1)
                act.activation(gate_a, bank[2][:, :], ACTF.Tanh, scale=rstd_a(b, 1)).then_inc(za_tanh_set, 1)
                act.activation(bank[0][:, :], bank[0][:, :], ACTF.Gelu_apprx_tanh, scale=rstd_a(b, 0)).then_inc(u_act_set, 1)

            def turned_hi_y(p, b):
                n = index_a(p, b)
                for half in range(2):
                    act.wait_ge(y_turned, 2 * n + 1 + half)
                    copy(yt_a[:, 0, 4 * half:4 * half + 4, :],
                         bank[5 + half][:, :].rearrange("p (k t) -> p k t", k=4)).then_inc(yt_hi_set, 1)

            def step_a(p, b):
                now, ahead, behind = (p, b), later_a(p, b, 1), later_a(p, b, -1)
                if exists_a(*behind):
                    turned_hi_y(*behind)
                if exists_a(*now):
                    leave_projection_a(*now)
                if exists_a(*ahead):
                    turned_hi_a(*ahead)

            act.wait_ge(projected, NB)
            for k in range(KT):
                j = k if k < 4 else k % 2
                act.wait_ge(wa_in[j], 16 if k < 4 else 32 if k < 6 else 48)
                source = (stage_a if k < 2 or k >= 4 else stage_c)[:, k % 2, :]
                copy(wa_hi[:, k, :], source, gain[:, k:k + 1]).then_inc(wa_hi_set, 1)
            turned_hi_a(0, 0)
            act.wait_ge(yb_set, NB)
            for j in range(2):
                act.wait_ge(yb_stored[j], 16 * (NB // 2))
            act.wait_ge(wa_lo_set, KT)
            for k in range(KT):
                act.wait_ge(wo_in[k % 2], 16 * (k // 2) + 16)
                copy(wo_hi[:, k, :], wo_stage[k % 2]).then_inc(wo_hi_set, 1)
            act.wait_ge(wo_lo_set, KT)
            run_a(act, step_a)

        @block.vector
        def _(dve):
            def turned_lo(p, b):
                n = index(p, b)
                for half in range(2):
                    dve.wait_ge(xt_hi_set, 2 * n + 1 + half)
                    dve.tensor_tensor(xt[:, b, 1, 4 * half:4 * half + 4, :],
                                      bank[T_BANK + half][:, :].rearrange("p (k t) -> p k t", k=4),
                                      xt[:, b, 0, 4 * half:4 * half + 4, :].bitcast(F32), ALU.subtract).then_inc(xt_lo_set, 1)

            STEPS_X = 3 + RSQRT_STEPS

            def rms_of_x(p, b):
                n = index(p, b)
                base = STEPS_X * n
                dve.wait_ge(x_in[b], 16 * p + 16)
                dve.bn_stats(stats[:, 0, :], xs[:, b, 0:HALF])
                dve.bn_stats(stats[:, 1, :], xs[:, b, HALF:D]).then_inc(x_read, 1)
                dve.wait_ge(x_read, n + 1)
                dve.memset(newton, 0.0)
                dve.bn_aggr(mean_var, stats[:, :, :]).then_inc(stats_steps, 1)
                dve.wait_ge(stats_steps, base + 1)
                dve.scalar_tensor_tensor(out=mean_sq, in0=mean_var[:, 0:1], scalar=mean_var[:, 0:1],
                                         in1=mean_var[:, 1:2], op0=ALU.mult, op1=ALU.add).then_inc(stats_steps, 1)
                dve.wait_ge(stats_steps, base + 2)
                dve.tensor_scalar(mean_sq, mean_sq, NORM_EPS, None, ALU.add).then_inc(stats_steps, 1)
                dve.wait_ge(stats_steps, base + 3)
                rsqrt(dve, stats_steps, base + 3, mean_sq, rstd_b(b, 0), newton)
                dve.tensor_scalar(rstd_b(b, 1), rstd_b(b, 0), float(HD) ** -0.5, None, ALU.mult)
                dve.tensor_scalar(rstd_b(b, 2), rstd_b(b, 0), 0.5, None, ALU.mult)
                column = rstd_all[:, n:n + 1] if isinstance(n, int) else rstd_all[:, bass.ds(n, 1)]
                dve.tensor_copy(column, rstd_b(b, 0)).then_inc(rstd_set, 1)

            def leave_projection(p, b):
                n = index(p, b)
                dve.wait_ge(q_hi_set, n + 1)
                dve.scalar_tensor_tensor(out=q_tok[:, :, 1, :].bitcast(F32R),
                                         in0=bank[Q_BANK][:, :].rearrange("p (h d) -> p h d", h=H), scalar=rstd_b(b, 1),
                                         in1=q_tok[:, :, 0, :], op0=ALU.mult, op1=ALU.subtract).then_inc(q_lo_set, 1)
                dve.wait_ge(z_tanh_set, n + 1)
                dve.tensor_scalar(gate_b[:, b, :], gate_b[:, b, :], 1.0, rstd_b(b, 2), ALU.add, ALU.mult).then_inc(gate_steps, 1)
                dve.wait_ge(gate_steps, n + 1)
                dve.tensor_tensor(gate_b[:, b, :], bank[Z_BANK][:, :], gate_b[:, b, :], ALU.mult).then_inc(gate_b_set, 1)
                dve.wait_ge(v_set, n + 1)
                for c in range(2):
                    last = dve.scalar_tensor_tensor(out=k_tok[:, 1, :, c, :].bitcast(F32R),
                                                    in0=bank[KV_BANK][:, 0:KVW].rearrange("p (g d) -> p g d", g=G),
                                                    scalar=rstd_b(b, 0), in1=k_tok[:, 0, :, 0, :],
                                                    op0=ALU.mult, op1=ALU.subtract)
                last.then_inc(k_lo_set, 1)

            STEPS_S = 5

            def soft_max(p, b):
                n = index(p, b)
                base = STEPS_S * n
                keys = P if isinstance(n, int) and n == 0 else 2 * P
                at = P if b == 0 else 0
                for half in range(2):
                    part = slice(4 * half, 4 * half + 4)
                    for j in range(2 * half, 2 * half + 2):
                        dve.wait_ge(scored, 4 * n + j + 1)
                        last = dve.tensor_tensor(probs[:, 2 * j:2 * j + 2, 0:keys],
                                                 bank[T_BANK + j][:, :].rearrange("p (h k) -> p h k", h=2)[:, :, 0:keys],
                                                 bias[:, 2 * j:2 * j + 2, at:at + keys], ALU.add)
                    last.then_inc(softmax_steps, 1)
                    dve.wait_ge(softmax_steps, base + 2 * half + 1)
                    dve.tensor_reduce(row_max[:, part], probs[:, part, 0:keys], mybir.AxisListType.X, ALU.max).then_inc(softmax_steps, 1)
                    dve.wait_ge(softmax_steps, base + 2 * half + 2)
                    negated = dve.scalar_tensor_tensor(out=neg_max[:, part], in0=row_max[:, part], scalar=-1.0,
                                                       in1=neg_sink[:, part], op0=ALU.mult, op1=ALU.min)
                    negated.then_inc(softmax_steps if half else max_set, 1)
                dve.wait_ge(softmax_steps, base + 5)
                dve.tensor_tensor(sink_diff, neg_max, neg_sink[:, :], ALU.subtract).then_inc(max_set, 1)

            def leave_probs(p, b):
                n = index(p, b)
                used = 1 if isinstance(n, int) and n == 0 else 2
                for j in (1, 3):
                    dve.wait_ge(p_turned, 4 * n + 1 + j)
                    dve.tensor_copy(probs_t[:, 2 * j:2 * j + 2, 0:used, :],
                                    bank[T_BANK + j][:, :].rearrange("p (h s t) -> p h s t", h=2, s=2)[:, :, 0:used, :]).then_inc(p_copied_dve, 1)

            def denominators(p, b):
                n = index(p, b)
                dve.wait_ge(sink_exp_set, n + 1)
                dve.tensor_tensor(row_sum, row_sum, sink_exp, ALU.add).then_inc(denominator_steps, 1)
                dve.wait_ge(denominator_steps, 2 * n + 1)
                dve.reciprocal(row_inv, row_sum).then_inc(denominator_steps, 1)
                dve.wait_ge(denominator_steps, 2 * n + 2)

            def gate(p, b):
                n = index(p, b)
                dve.wait_ge(attended, n + 1)
                ge(dve, yb_stored[b], 16 * p)
                dve.tensor_tensor(y_b[:, b, :].rearrange("p (h d) -> p h d", h=H),
                                  bank[O_BANK][:, :].rearrange("p (h d) -> p h d", h=H),
                                  row_inv.unsqueeze(2).to_broadcast([P, H, HD]), ALU.mult).then_inc(o_read, 1)
                dve.wait_ge(o_read, n + 1)
                dve.tensor_tensor(y_b[:, b, :], y_b[:, b, :], gate_b[:, b, :], ALU.mult).then_inc(yb_set, 1)

            def step(p, b):
                ahead, behind, last = later(p, b, 1), later(p, b, -1), later(p, b, -2)
                if exists(*behind):
                    leave_projection(*behind)
                if exists(*last):
                    gate(*last)
                if exists(*ahead):
                    turned_lo(*ahead)
                    rms_of_x(*ahead)
                if exists(*behind):
                    soft_max(*behind)
                    leave_probs(*behind)
                    denominators(*behind)

            
            dve.memset(bias_rows[:, :, :], MASKED).then_inc(rows_set, 1)
            dve.wait_ge(buckets_in, 16 * 2)
            for h in range(H):
                dve.tensor_scalar(rel_rows[:, h, :], onehot, rel[:, h:h + 1], None, ALU.mult).then_inc(rel_spread, 1)
            turned_lo(0, 0)
            dve.wait_ge(rel_summed, 2)
            dve.wait_ge(rows_set, 1)
            dve.tensor_copy(bias_rows[:, 0:4, P:2 * P], bank[5][:, :].rearrange("p (h j) -> p h j", h=4))
            dve.tensor_copy(bias_rows[:, 4:8, P:2 * P], bank[6][:, :].rearrange("p (h j) -> p h j", h=4)).then_inc(rows_set, 1)
            dve.wait_ge(consts_in, 16 * 5)
            dve.tensor_scalar(neg_sink[:, :], neg_sink[:, :], -1.0, None, ALU.mult).then_inc(sink_negated, 1)
            dve.wait_ge(sink_negated, 1)
            for k in range(KT):
                dve.wait_ge(wb_hi_set, k + 1)
                dve.scalar_tensor_tensor(out=wb_lo[:, k, :], in0=stage_b[:, k, :], scalar=gain[:, k:k + 1],
                                         in1=wb_hi[:, k, :].bitcast(F32), op0=ALU.mult, op1=ALU.subtract).then_inc(wb_lo_set, 1)
            rms_of_x(0, 0)
            dve.wait_ge(bias_in, 32)
            run_b(dve, step)

            def turned_lo_a(p, b):
                n = index_a(p, b)
                for half in range(2):
                    dve.wait_ge(xa_hi_set, 2 * n + 1 + half)
                    dve.tensor_tensor(xt_a[:, 1, 4 * half:4 * half + 4, :],
                                      bank[5 + half][:, :].rearrange("p (k t) -> p k t", k=4),
                                      xt_a[:, 0, 4 * half:4 * half + 4, :].bitcast(F32), ALU.subtract).then_inc(xa_lo_set, 1)

            def rstd_of_pass_b(p, b):
                n = index_a(p, b)
                column = rstd_all[:, n:n + 1] if isinstance(n, int) else rstd_all[:, bass.ds(n, 1)]
                dve.tensor_copy(rstd_a(b, 0), column).then_inc(rstd_a_steps, 1)
                dve.wait_ge(rstd_a_steps, n + 1)
                dve.tensor_scalar(rstd_a(b, 1), rstd_a(b, 0), 0.5, None, ALU.mult).then_inc(rstd_a_set, 1)

            STEPS_LN = 5 + RSQRT_STEPS

            def layer_norm(p, b):
                n = index_a(p, b)
                base = STEPS_LN * n
                done = 0

                def link(ins, then_aggregate=False):
                    nonlocal done
                    done += 1
                    ins.then_inc(ln_steps, 1)
                    dve.wait_ge(ln_steps, base + done)
                    if then_aggregate:
                        dve.memset(newton, 0.0)

                dve.wait_ge(v_act_set, n + 1)
                link(dve.bn_stats(stats[:, 0, :], v_act), then_aggregate=True)
                link(dve.bn_aggr(mean_var, stats[:, 0:1, :]))
                link(dve.tensor_scalar(mean_sq, mean_var[:, 1:2], NORM_EPS, None, ALU.add))
                rsqrt(dve, ln_steps, base + done, mean_sq, rstd_ln, newton)
                done += RSQRT_STEPS
                link(dve.tensor_scalar(v_act, v_act, mean_var[:, 0:1], rstd_ln, ALU.subtract, ALU.mult))
                link(dve.tensor_tensor(v_act, v_act, ln_gain[:, :], ALU.mult))
                dve.tensor_tensor(v_act, v_act, ln_bias[:, :], ALU.add).then_inc(vn_set, 1)
                assert done == STEPS_LN

            def gate_of_a(p, b):
                n = index_a(p, b)
                dve.wait_ge(za_tanh_set, n + 1)
                dve.tensor_scalar(gate_a, gate_a, 1.0, rstd_a(b, 1), ALU.add, ALU.mult).then_inc(gate_a_steps, 1)
                dve.wait_ge(gate_a_steps, n + 1)
                dve.tensor_tensor(gate_a, bank[2][:, :], gate_a, ALU.mult).then_inc(z_read, 1)
                dve.wait_ge(z_read, n + 1)
                dve.wait_ge(u_act_set, n + 1)
                dve.tensor_tensor(gate_a, bank[0][:, :], gate_a, ALU.mult).then_inc(u_read, 1)

            def gate_mixed(p, b):
                n = index_a(p, b)
                dve.wait_ge(mixed, n + 1)
                dve.tensor_tensor(v_act.rearrange("p (g d) -> p g d", g=AG),
                                  bank[O_BANK][:, :].rearrange("p (g d) -> p g d", g=AG),
                                  bs_t[:, :].unsqueeze(2).to_broadcast([P, AG, AD]), ALU.add).then_inc(ya_steps, 1)
                dve.wait_ge(ya_steps, n + 1)
                dve.wait_ge(u_read, n + 1)
                dve.tensor_tensor(gate_a, gate_a, v_act, ALU.mult).then_inc(ya_set, 1)
                dve.wait_ge(ya_set, n + 1)

            def turned_lo_y(p, b):
                n = index_a(p, b)
                for half in range(2):
                    dve.wait_ge(yt_hi_set, 2 * n + 1 + half)
                    dve.tensor_tensor(yt_a[:, 1, 4 * half:4 * half + 4, :],
                                      bank[5 + half][:, :].rearrange("p (k t) -> p k t", k=4),
                                      yt_a[:, 0, 4 * half:4 * half + 4, :].bitcast(F32), ALU.subtract).then_inc(yt_lo_set, 1)

            STEPS_POST = 7 + RSQRT_STEPS

            def post_norm(p, b):
                n = index_a(p, b)
                base = STEPS_POST * n
                done = 0

                def link(ins, then_aggregate=False):
                    nonlocal done
                    done += 1
                    ins.then_inc(post_steps, 1)
                    dve.wait_ge(post_steps, base + done)
                    if then_aggregate:
                        dve.memset(newton, 0.0)

                dve.wait_ge(y_projected, n + 1)
                dve.bn_stats(stats[:, 0, :], bank[3][:, :])
                link(dve.bn_stats(stats[:, 1, :], bank[4][:, :]), then_aggregate=True)
                link(dve.bn_aggr(mean_var, stats[:, :, :]))
                link(dve.scalar_tensor_tensor(out=mean_sq, in0=mean_var[:, 0:1], scalar=mean_var[:, 0:1],
                                              in1=mean_var[:, 1:2], op0=ALU.mult, op1=ALU.add))
                link(dve.tensor_scalar(mean_sq, mean_sq, NORM_EPS, None, ALU.add))
                rsqrt(dve, post_steps, base + done, mean_sq, rstd_post, newton)
                done += RSQRT_STEPS
                for half in range(2):
                    part = slice(half * HALF, (half + 1) * HALF)
                    link(dve.scalar_tensor_tensor(out=v_act, in0=bank[3 + half][:, :], scalar=rstd_post,
                                                  in1=post_gain[:, part], op0=ALU.mult, op1=ALU.mult))
                    last = dve.tensor_tensor(xs[:, b, part], xs[:, b, part], v_act, ALU.add)
                    if half == 0:
                        link(last)
                last.then_inc(post_set, 1)
                assert done == STEPS_POST

            def step_a(p, b):
                now, ahead, behind = (p, b), later_a(p, b, 1), later_a(p, b, -1)
                if exists_a(*behind):
                    turned_lo_y(*behind)
                if exists_a(*now):
                    layer_norm(*now)
                    gate_of_a(*now)
                if exists_a(*ahead):
                    turned_lo_a(*ahead)
                    rstd_of_pass_b(*ahead)
                if exists_a(*now):
                    gate_mixed(*now)
                if exists_a(*behind):
                    post_norm(*behind)

            for k in range(KT):
                dve.wait_ge(wa_hi_set, k + 1)
                ge(dve, wa_lo_set, k)
                source = (stage_a if k < 2 or k >= 4 else stage_c)[:, k % 2, :]
                dve.scalar_tensor_tensor(out=wa_lo[:, k, :], in0=source, scalar=gain[:, k:k + 1],
                                         in1=wa_hi[:, k, :].bitcast(F32), op0=ALU.mult, op1=ALU.subtract).then_inc(wa_lo_set, 1)
            turned_lo_a(0, 0)
            rstd_of_pass_b(0, 0)
            dve.wait_ge(wa_lo_set, KT)
            for k in range(KT):
                dve.wait_ge(wo_hi_set, k + 1)
                dve.tensor_tensor(wo_lo[:, k, :], wo_stage[k % 2], wo_hi[:, k, :].bitcast(F32), ALU.subtract).then_inc(wo_lo_set, 1)
            dve.wait_ge(wo_lo_set, KT)
            run_a(dve, step_a)


def kernel(x, pre_norm_g, w_in, ln_v_g, ln_v_b, w_spatial, b_spatial, sinks, rel_bias, w_out, post_norm_g):
    import concourse.bacc as bacc
    from concourse.bass_utils import run_bass_kernel_spmd

    buckets = rel_bias.shape[0]
    distance = np.arange(P - 1, -1, -1)
    exact = buckets // 2
    far = exact + (np.log(np.maximum(distance, 1) / exact) / math.log(REL_MAX_DIST / exact) * (buckets - exact)).astype(np.int32)
    bucket = np.where(distance < exact, distance, np.minimum(far, buckets - 1))
    onehot = np.equal(np.arange(buckets)[:, None], bucket[None, :]).astype(np.float32)

    arrays = {
        "x": x, "pre_norm_g": pre_norm_g.reshape(-1, P).T, "w_in": w_in, "ln_v_g": ln_v_g, "ln_v_b": ln_v_b,
        "w_spatial": w_spatial[0].transpose(2, 0, 1), "b_spatial": b_spatial[0].T, "sinks": sinks, "rel_bias": rel_bias,
        "w_out": w_out, "post_norm_g": post_norm_g, "bucket_onehot": onehot, "identity": np.eye(P, dtype=np.float32),
    }
    arrays = {f"in_{name}": np.ascontiguousarray(a) for name, a in arrays.items()}
    nc = bacc.Bacc("TRN2", target_bir_lowering=False, num_devices=1)
    args = [nc.dram_tensor(name, a.shape, mybir.dt.from_np(a.dtype), kind="ExternalInput").ap() for name, a in arrays.items()]
    out = nc.dram_tensor("out", x.shape, F32, kind="ExternalOutput").ap()
    build(nc, *args, out)
    result = run_bass_kernel_spmd(nc, [arrays], core_ids=[0])
    return result.results[0]["out"]
```

```python
from contextlib import ExitStack
import math

import numpy as np
import concourse.bass as bass
from concourse import mybir

F32 = mybir.dt.float32
F32R = mybir.dt.float32r
I32 = mybir.dt.int32
ALU = mybir.AluOpType
ACTF = mybir.ActivationFunctionType

P = 128
MASKED = -1e30
NORM_EPS = 1e-6
REL_MAX_DIST = 128
STATS = 6
HALF = 512
RSQRT_STEPS = 10
X_SLOTS = 3


def ge(eng, sem, value):
    if isinstance(value, int) and value <= 0:
        return
    eng.wait_ge(sem, value)


def rsqrt(dve, sem, base, x, y, tmp):
    done = 0

    def link(ins):
        nonlocal done
        done += 1
        ins.then_inc(sem, 1)
        dve.wait_ge(sem, base + done)

    link(dve.tensor_scalar(y.bitcast(I32), x.bitcast(I32), -0.5, 1597463007.0, ALU.mult, ALU.add))
    for _ in range(3):
        link(dve.scalar_tensor_tensor(out=tmp, in0=y, scalar=y, in1=x, op0=ALU.mult, op1=ALU.mult))
        link(dve.tensor_scalar(tmp, tmp, -0.5, 1.5, ALU.mult, ALU.add))
        link(dve.tensor_tensor(y, y, tmp, ALU.mult))
    assert done == RSQRT_STEPS


def build(nc, x, x_t, pre_g, w_in, ln_g, ln_b, w_spatial, b_spatial, sinks, rel_bias, w_out, post_g,
          bucket_onehot, identity, out):
    _, SEQ, D = x.shape
    AW = ln_g.shape[1]
    AG = w_spatial.shape[1]
    AD = AW // AG
    H = sinks.shape[1]
    BUCKETS = rel_bias.shape[0]
    HD = (w_out.shape[1] - AW) // H
    BW = H * HD
    KVW = (w_in.shape[2] - 3 * AW - 2 * BW) // 2
    G = KVW // HD
    GH = H // G
    NB = SEQ // P
    KT = D // P
    BCOLS = 2 * BW + 2 * KVW
    ACOLS = 3 * AW
    assert D == 2 * HALF and AW == HALF and BW == HALF and HD == 64 and H == 8 and G == 2 and NB == 32

    y_scratch = nc.dram_tensor("y_b_scratch", [NB, P, BW], F32, kind="Internal").ap()
    PITCH = 3 * P
    bias_scratch = nc.dram_tensor("bias_scratch", [H, P, PITCH], F32, kind="Internal")

    x_blocks = x.rearrange("o (n p) d -> (o n) p d", p=P)
    out_blocks = out.rearrange("o (n p) d -> (o n) p d", p=P)

    ctx = ExitStack()
    with ctx:
        def sb(stack, name, shape, dt=F32):
            return stack.enter_context(nc.sbuf_tensor(name, shape, dt))

        ident = sb(ctx, "ident", [P, P])
        post_gain = sb(ctx, "post_gain", [P, D])
        ln_gain = sb(ctx, "ln_gain", [P, AW])
        ln_bias = sb(ctx, "ln_bias", [P, AW])
        ws_t = sb(ctx, "ws_t", [P, AG, P])
        bs_t = sb(ctx, "bs_t", [P, AG])
        gain = sb(ctx, "gain", [P, KT])
        neg_sink = sb(ctx, "neg_sink", [P, H])
        rstd_all = sb(ctx, "rstd_all", [P, NB])
        small = sb(ctx, "small", [P, 32])
        stats = sb(ctx, "stats", [P, 2, STATS])
        xs = sb(ctx, "xs", [P, X_SLOTS, D])
        act_buf = sb(ctx, "act_buf", [P, 3, HALF])
        over = ExitStack()
        xt_raw = sb(over, "xt_raw", [P, 2, 2, KT, P])
        over.close()
        xt = sb(ctx, "xt", [P, 2, 2, KT, P], F32R)

        over = ExitStack()
        wb_hi = sb(over, "wb_hi", [P, KT, BCOLS], F32R)
        wb_lo = sb(over, "wb_lo", [P, KT, BCOLS], F32R)
        over.close()
        over = ExitStack()
        sb(over, "under_wb_raw", [P, KT, BCOLS])
        wb_raw = sb(over, "wb_raw", [P, KT, BCOLS])
        over.close()
        over = ExitStack()
        sb(over, "under_wa_raw", [P, KT, ACOLS])
        wa_raw = sb(over, "wa_raw", [P, KT, ACOLS])
        over.close()
        wa_hi = sb(ctx, "wa_hi", [P, KT, ACOLS], F32R)
        wa_lo = sb(ctx, "wa_lo", [P, KT, ACOLS], F32R)

        work = ExitStack()
        probs = sb(work, "probs", [P, H, 2 * P])
        probs_t = sb(work, "probs_t", [P, H, 2, P])
        k_stack = sb(work, "k_stack", [P, 2 * G, 2, P], F32R)
        y_b = sb(work, "y_b", [P, 2, BW])
        gate_b = sb(work, "gate_b", [P, 2, BW])
        k_tok = sb(work, "k_tok", [P, 2, G, 2, HD])
        v_tok = sb(work, "v_tok", [P, 2, KVW])
        row = sb(work, "row", [P, 6, H])
        filled = 4 * H * P + 2 * G * 2 * P + 4 * BW + 4 * G * HD + 2 * KVW + 6 * H
        assert filled <= KT * D
        if filled < KT * D:
            sb(work, "pad", [P, KT * D - filled])
        wa_stage = sb(work, "wa_stage", [P, 2, ACOLS])
        q_tok = sb(work, "q_tok", [P, H, 2, HD])
        q_stack = sb(work, "q_stack", [P, H, P], F32R)
        bias = sb(work, "bias", [P, H, 3 * P])
        work.close()
        over = ExitStack()
        sb(over, "under_wo_raw", [P, KT, D])
        wo_raw = sb(over, "wo_raw", [P, KT, D])
        over.close()
        wo_hi = sb(ctx, "wo_hi", [P, KT, D], F32R)
        wo_lo = sb(ctx, "wo_lo", [P, KT, D], F32R)

        row_max, neg_max, sink_diff, row_sum, sink_exp, row_inv = (row[:, j, :] for j in range(6))
        mean_var = small[:, 0:2]
        mean_sq, newton = small[:, 2:3], small[:, 3:4]
        rstd_ln, rstd_post = small[:, 4:5], small[:, 5:6]

        def mean_sq_x(slot):
            return small[:, 22 + slot:23 + slot]

        def rstd_b(slot, j):
            return small[:, 8 + 3 * slot + j:9 + 3 * slot + j]

        def rstd_a(slot, j):
            return small[:, 16 + 2 * slot + j:17 + 2 * slot + j]

        v_act, gate_a, yb_in = (act_buf[:, j, :] for j in range(3))
        xt_a, yt_a = xt[:, 0], xt[:, 1]
        squares = act_buf[:, 0:2, :].rearrange("p a b -> p (a b)")
        rel_rows = probs[0:BUCKETS, 0:4, :].rearrange("p h (c j) -> p (h c) j", c=2)
        onehot = probs_t[0:BUCKETS, 0, 0, :]
        ones = probs_t[0:BUCKETS, 0, 1, :]
        rel = probs_t[0:BUCKETS, 1, 0, 0:H]
        bias_rows = wa_stage[:, :, :].rearrange("p a b -> p (a b)").rearrange("p (h j) -> p h j", h=H)

        bank = [ctx.enter_context(nc.psum_tensor(f"bank{j}", [P, HALF], F32)) for j in range(8)]
        Q_BANK, KV_BANK, Z_BANK, T_BANK, O_BANK = 0, 1, 2, 3, 7

        def sem(name):
            return ctx.enter_context(nc.semaphore(name))

        ident_in, gain_in, consts_in, ws_in, buckets_in, bias_out, bias_in = (sem(s) for s in (
            "ident_in", "gain_in", "consts_in", "ws_in", "buckets_in", "bias_out", "bias_in"))
        ones_set, rel_spread, rel_summed, rows_set, sink_negated = (sem(s) for s in (
            "ones_set", "rel_spread", "rel_summed", "rows_set", "sink_negated"))
        ws_masked = sem("ws_masked")
        wb_in = [sem(f"wb_in{k}") for k in range(KT)]
        wa_in = [sem(f"wa_in{k}") for k in range(KT)]
        wo_in = [sem(f"wo_in{k}") for k in range(KT)]
        wb_used = sem("wb_used")
        wb_hi_set, wb_lo_set, wa_hi_set, wa_lo_set, wo_hi_set, wo_lo_set = (sem(s) for s in (
            "wb_hi_set", "wb_lo_set", "wa_hi_set", "wa_lo_set", "wo_hi_set", "wo_lo_set"))
        x_in = [sem(f"x_in{j}") for j in range(2)]
        xt_in = [sem(f"xt_in{j}") for j in range(2)]
        xt_hi_set, xt_lo_set, x_squared, rstd_set = (sem(s) for s in (
            "xt_hi_set", "xt_lo_set", "x_squared", "rstd_set"))
        projected, q_hi_set, k_hi_set, v_set, z_tanh_set, q_lo_set, k_lo_set, gate_b_set = (sem(s) for s in (
            "projected", "q_hi_set", "k_hi_set", "v_set", "z_tanh_set", "q_lo_set", "k_lo_set", "gate_b_set"))
        qk_turned, stacked, scored, max_set, exp_set, sink_exp_set = (sem(s) for s in (
            "qk_turned", "stacked", "scored", "max_set", "exp_set", "sink_exp_set"))
        p_turned, p_copied_act, p_copied_dve, attended, o_read, yb_set = (sem(s) for s in (
            "p_turned", "p_copied_act", "p_copied_dve", "attended", "o_read", "yb_set"))
        yb_stored = [sem(f"yb_stored{j}") for j in range(2)]
        stats_steps, softmax_steps, gate_steps, denominator_steps = (sem(s) for s in (
            "stats_steps", "softmax_steps", "gate_steps", "denominator_steps"))
        xa_in = [sem(f"xa_in{j}") for j in range(X_SLOTS)]
        yb_loaded = sem("yb_loaded")
        xta_in, xa_hi_set, xa_lo_set, rstd_a_set = (sem(s) for s in (
            "xta_in", "xa_hi_set", "xa_lo_set", "rstd_a_set"))
        a_projected, v_act_set, za_tanh_set, u_act_set, z_read, u_read, vn_set = (sem(s) for s in (
            "a_projected", "v_act_set", "za_tanh_set", "u_act_set", "z_read", "u_read", "vn_set"))
        mixed, ya_set, y_turned, yt_hi_set, yt_lo_set, y_projected, post_set = (sem(s) for s in (
            "mixed", "ya_set", "y_turned", "yt_hi_set", "yt_lo_set", "y_projected", "post_set"))
        out_stored = [sem(f"out_stored{j}") for j in range(X_SLOTS)]
        ln_steps, gate_a_steps, post_steps, rstd_a_steps, ya_steps = (sem(s) for s in (
            "ln_steps", "gate_a_steps", "post_steps", "rstd_a_steps", "ya_steps"))

        def later(p, b, d):
            return p + (b + d) // 2, (b + d) % 2

        def index(p, b):
            return 2 * p + b

        def exists(p, b):
            n = index(p, b)
            return not isinstance(n, int) or 0 <= n < NB

        def run_b(eng, step):
            for s in range(3):
                step(s // 2, s % 2)
            with eng.Fori(0, (NB - 4) // 2) as i:
                step(i + 1, 1)
                step(i + 2, 0)
            step((NB - 1) // 2, (NB - 1) % 2)

        def later_a(p, b, d):
            return p + (b + d) // 3, (b + d) % 3

        def index_a(p, b):
            return 3 * p + b

        def exists_a(p, b):
            n = index_a(p, b)
            return not isinstance(n, int) or 0 <= n < NB

        def run_a(eng, step):
            step(0, 2)
            with eng.Fori(1, (NB - 2) // 3) as i:
                step(i, 0)
                step(i, 1)
                step(i, 2)
            for s in range(NB - 2, NB + 1):
                step(s // 3, s % 3)

        def xt_of(n):
            return xt[:, 1] if isinstance(n, int) and n == 1 else xt[:, 0]

        def row_of(blocks, n):
            if isinstance(n, int):
                return blocks[n]
            return blocks[bass.ds(n, 1)].rearrange("n p d -> p (n d)")

        block = ctx.enter_context(nc.Block())

        w_rows = w_in[0].rearrange("(k p) c -> k p c", p=P)
        wo_rows = w_out[0].rearrange("(k p) c -> k p c", p=P)
        def reach(last_value, first_tile):
            return min(KT, -(-(last_value - first_tile * BCOLS) // BCOLS))

        def hi_after(k):
            end = (k + 1) * ACOLS
            if k * ACOLS >= KT * BCOLS:
                return reach(end, KT)
            return KT if end > KT * BCOLS else reach(end, 0)

        def lo_after(k):
            if (KT + k) * ACOLS >= 2 * KT * BCOLS:
                return 0
            return reach((KT + k + 1) * ACOLS, KT)

        BESIDE = [k for k in range(KT) if lo_after(k) == 0]
        FIRST_USED = [0, KT - 1, 1] + [k for k in range(2, KT - 1) if k in BESIDE] + [
            k for k in range(2, KT - 1) if k not in BESIDE]
        STAGED = (0, 1)

        def wait_wb_used(eng, tiles):
            if tiles == KT:
                eng.wait_ge(projected, NB)
            elif tiles > 0:
                eng.wait_ge(wb_used, tiles)

        def row_of_t(n):
            if isinstance(n, int):
                return x_t[n]
            return x_t[bass.ds(n, 1)].rearrange("n p k t -> p (n k) t")

        @block.sync
        def _(sp):
            sp.dma_start(onehot, bucket_onehot).then_inc(buckets_in, 16)
            sp.dma_start(rel, rel_bias).then_inc(buckets_in, 16)
            sp.dma_start(gain[:, :], pre_g).then_inc(gain_in, 16)
            for k in range(KT):
                sp.dma_start(wb_raw[:, k, :], w_rows[k, :, ACOLS:]).then_inc(wb_in[k], 16)
                if k == 0:
                    sp.dma_start(xt_raw[:, 0, 1], row_of_t(0)).then_inc(xt_in[0], 16)
            sp.dma_start(xs[:, 0, :], x_blocks[0]).then_inc(x_in[0], 16)
            sp.dma_start(ident[:, :], identity).then_inc(ident_in, 16)
            sp.dma_start(xt_raw[:, 1, 1], row_of_t(1)).then_inc(xt_in[1], 16)
            sp.dma_start(xs[:, 1, :], x_blocks[1]).then_inc(x_in[1], 16)

            def step(p, b):
                pp, slot = later(p, b, 1)
                if exists(pp, slot) and exists(*later(p, b, -1)):
                    n = index(p, b)
                    sp.wait_ge(projected, n)
                    sp.dma_start(xt_raw[:, slot, 1], row_of_t(n + 1)).then_inc(xt_in[slot], 16)
                    sp.wait_ge(x_squared, n)
                    sp.dma_start(xs[:, slot, :], row_of(x_blocks, n + 1)).then_inc(x_in[slot], 16)
                if exists(*later(p, b, -2)):
                    n = index(p, b) - 2
                    sp.wait_ge(yb_set, n + 1)
                    sp.dma_start(row_of(y_scratch, n), y_b[:, b, :]).then_inc(yb_stored[b], 16)

            def step_b(p, b):
                s = index(p, b)
                if isinstance(s, int) and s == NB - 1:
                    sp.wait_ge(projected, NB - 1)
                    sp.dma_start(xt_raw[:, 0, 1], row_of_t(0)).then_inc(xta_in, 16)
                    sp.wait_ge(bias_out, 16)
                    for k in STAGED:
                        sp.dma_start(wa_stage[:, k, :], w_rows[k, :, 0:ACOLS]).then_inc(wa_in[k], 16)
                    for k in BESIDE:
                        sp.dma_start(wa_raw[:, k, :], w_rows[k, :, 0:ACOLS]).then_inc(wa_in[k], 16)
                step(p, b)

            run_b(sp, step_b)
            for k in range(KT):
                if k not in BESIDE and k not in STAGED:
                    wait_wb_used(sp, lo_after(k))
                    sp.dma_start(wa_raw[:, k, :], w_rows[k, :, 0:ACOLS]).then_inc(wa_in[k], 16)
            sp.wait_ge(projected, NB)
            sp.wait_ge(xta_in, 16)
            sp.dma_start(xt_raw[:, 1, 1], row_of_t(1)).then_inc(xta_in, 16)
            sp.wait_ge(x_squared, NB)
            for j in range(2):
                sp.dma_start(xs[:, j, :], x_blocks[j]).then_inc(xa_in[j], 16)
            sp.wait_ge(yb_set, NB - 1)
            sp.dma_start(y_scratch[NB - 2], y_b[:, 0, :]).then_inc(yb_stored[0], 16)
            sp.wait_ge(yb_stored[0], 16 * (NB // 2))
            sp.dma_start(yb_in, y_scratch[0]).then_inc(yb_loaded, 16)
            sp.wait_ge(scored, 4 * NB)
            sp.wait_ge(wa_lo_set, 3)
            for k in range(KT):
                if k == KT - 3:
                    sp.wait_ge(max_set, 2 * NB)
                sp.dma_start(wo_raw[:, k, :], wo_rows[k]).then_inc(wo_in[k], 16)
            sp.wait_ge(yb_set, NB)
            sp.dma_start(y_scratch[NB - 1], y_b[:, 1, :]).then_inc(yb_stored[1], 16)
            sp.wait_ge(yb_stored[1], 16 * (NB // 2))

            def step_a(p, b):
                n = index_a(p, b)
                if exists_a(p, b):
                    sp.wait_ge(y_turned, 2 * n)
                    sp.dma_start(yb_in, row_of(y_scratch, n)).then_inc(yb_loaded, 16)
                before, slot = later_a(p, b, -2)
                if exists_a(*later_a(p, b, 1)):
                    sp.wait_ge(a_projected, n + 1)
                    sp.dma_start(xt_raw[:, 0, 1], row_of_t(n + 1)).then_inc(xta_in, 16)
                    if exists_a(before, slot):
                        sp.wait_ge(out_stored[slot], 16 * before + 16)
                    sp.dma_start(xs[:, slot, :], row_of(x_blocks, n + 1)).then_inc(xa_in[slot], 16)
                _, slot = later_a(p, b, -1)
                sp.wait_ge(post_set, n)
                sp.dma_start(row_of(out_blocks, n - 1), xs[:, slot, :]).then_inc(out_stored[slot], 16)

            step_a(0, 1)
            run_a(sp, step_a)
            for j in range(X_SLOTS):
                sp.wait_ge(out_stored[j], 16 * len(range(j, NB, X_SLOTS)))

        @block.gpsimd
        def _(pool):
            pool.memset(ones, 1.0).then_inc(ones_set, 1)
            pool.memset(bias_rows, MASKED).then_inc(rows_set, 1)
            pool.dma_start(neg_sink[:, :], sinks[0].partition_broadcast(P)).then_inc(consts_in, 16)
            pool.dma_start(ws_t[:, :, :], w_spatial).then_inc(ws_in, 16)
            pool.wait_ge(wb_in[KT - 1], 16)
            pool.wait_ge(rows_set, 2)
            pool.dma_start(bias_scratch.ap().rearrange("h p j -> p h j"), bias_rows).then_inc(bias_out, 16)
            pool.wait_ge(bias_out, 16)
            for at, keys in ((0, 2 * P), (2 * P, P)):
                pool.dma_start(bias[:, :, at:at + keys],
                               bass.AP(bias_scratch, P - 1, [[PITCH - 1, P], [P * PITCH, H], [1, keys]])).then_inc(bias_in, 16)
            for target, source in ((post_gain, post_g[0]), (ln_gain, ln_g[0]), (ln_bias, ln_b[0])):
                pool.dma_start(target[:, :], source.partition_broadcast(P)).then_inc(consts_in, 16)
            pool.dma_start(bs_t[:, :], b_spatial).then_inc(consts_in, 16)
            pool.wait_ge(ws_in, 16)
            pool.affine_select(out=ws_t[:, :, :], in_=ws_t[:, :, :], compare_op=ALU.is_ge, fill=0.0, base=0,
                               pattern=[[0, AG], [1, P]], channel_multiplier=-1).then_inc(ws_masked, 1)

        @block.tensor
        def _(pe):
            def turn(target, source):
                return pe.transpose(target, source, ident[:, :])

            def project_k(p, b, k):
                n = index(p, b)
                if k == 0:
                    pe.wait_ge(xt_lo_set, n + 1)
                if isinstance(n, int) and n == 0:
                    pe.wait_ge(wb_lo_set, k + 1)
                cols = ((Q_BANK, 0, BW, q_lo_set), (Z_BANK, BW + 2 * KVW, BCOLS, gate_b_set),
                        (KV_BANK, BW, BW + 2 * KVW, v_set))
                for part in range(2):
                    for j, a, e, emptied in cols:
                        if k == 0 and part == 0:
                            ge(pe, emptied, n)
                        for w in (wb_hi, wb_lo)[:2 - part]:
                            last = pe.matmul(bank[j][:, 0:e - a], xt[:, b, part, k, :], w[:, k, a:e],
                                             start=(k == 0 and part == 0 and w is wb_hi),
                                             stop=(k == KT - 1 and part == 1))
                if k == KT - 1:
                    last.then_inc(projected, 1)
                elif isinstance(n, int) and n == NB - 1:
                    last.then_inc(wb_used, 1)

            def turn_qk(p, b):
                n = index(p, b)
                pe.wait_ge(q_lo_set, n + 1)
                pe.wait_ge(k_lo_set, n + 1)
                for h in range(H):
                    last = turn(bank[T_BANK + h // 4][:, (h % 4) * P:(h % 4 + 1) * P],
                                q_tok[:, h, :, :].rearrange("p a d -> p (a d)"))
                    if h % 4 == 3:
                        last.then_inc(qk_turned, 1)
                for j in range(2 * G):
                    last = turn(bank[T_BANK + 2][:, j * P:(j + 1) * P],
                                k_tok[:, j // G, j % G, :, :].rearrange("p a d -> p (a d)"))
                last.then_inc(qk_turned, 1)

            def first_block(p, b):
                n = index(p, b)
                return isinstance(n, int) and n == 0

            def score(p, b):
                n = index(p, b)
                keys = P if first_block(p, b) else 2 * P
                pe.wait_ge(stacked, 3 * n + 3)
                for h in range(H):
                    for part in range(2):
                        moving = k_stack[:, part * G + h // GH, :, :].rearrange("p s k -> p (s k)")
                        last = pe.matmul(bank[T_BANK + h // 2][:, (h % 2) * 2 * P:(h % 2) * 2 * P + keys],
                                         q_stack[:, h, :], moving[:, 0:keys],
                                         start=(part == 0), stop=(part == 1))
                    if h % 2 == 1:
                        last.then_inc(scored, 1)

            def turn_probs(p, b, half):
                n = index(p, b)
                for h in range(4 * half, 4 * half + 4):
                    pe.wait_ge(exp_set, 8 * n + h + 1)
                    for s in range(1 if first_block(p, b) else 2):
                        at = ((h % 2) * 2 + s) * P
                        last = turn(bank[T_BANK + h // 2][:, at:at + P], probs[:, h, s * P:(s + 1) * P])
                    if h % 2 == 1:
                        last.then_inc(p_turned, 1)

            def attend(p, b):
                n = index(p, b)
                pe.wait_ge(p_copied_act, 2 * n + 2)
                pe.wait_ge(p_copied_dve, 2 * n + 2)
                pe.wait_ge(v_set, n + 1)
                ge(pe, o_read, n)
                slots = range(1 if first_block(p, b) else 2)
                for h in range(H):
                    g = h // GH
                    for s in slots:
                        last = pe.matmul(bank[O_BANK][:, h * HD:(h + 1) * HD], probs_t[:, h, s, :],
                                         v_tok[:, s, g * HD:(g + 1) * HD],
                                         start=(s == 0), stop=(s == slots[-1]))
                last.then_inc(attended, 1)

            def step(p, b):
                now, behind, last = (p, b), later(p, b, -1), later(p, b, -2)
                if exists(*last):
                    attend(*last)
                for k in range(KT):
                    project_k(*now, k)
                    if exists(*behind):
                        if k == 0:
                            turn_qk(*behind)
                        if k == 2:
                            score(*behind)
                        if k == 5:
                            turn_probs(*behind, 0)
                        if k == 6:
                            turn_probs(*behind, 1)

            pe.wait_ge(ones_set, 1)
            pe.wait_ge(rel_spread, H)
            for half in range(2):
                pe.matmul(bank[5 + half][:, :], ones, rel_rows[:, 4 * half:4 * half + 4, :].rearrange("b h j -> b (h j)"),
                          start=True, stop=True).then_inc(rel_summed, 1)
            pe.wait_ge(ident_in, 16)
            run_b(pe, step)

            def project_a(p, b, k, first, last_tile):
                n = index_a(p, b)
                if first:
                    pe.wait_ge(xa_lo_set, n + 1)
                for part in range(2):
                    for j, emptied in ((1, v_act_set), (2, z_read), (0, u_read)):
                        if first and part == 0:
                            ge(pe, emptied, n)
                        for w in (wa_hi, wa_lo)[:2 - part]:
                            last = pe.matmul(bank[j][:, :], xt_of(n)[:, part, k, :], w[:, k, j * AW:(j + 1) * AW],
                                             start=(first and part == 0 and w is wa_hi),
                                             stop=(last_tile and part == 1))
                if last_tile:
                    last.then_inc(a_projected, 1)

            def turn_y(p, b):
                n = index_a(p, b)
                ge(pe, yt_lo_set, 2 * n)
                pe.wait_ge(ya_set, n + 1)
                for k in range(4):
                    last = turn(bank[5][:, k * P:(k + 1) * P], gate_a[:, k * P:(k + 1) * P])
                last.then_inc(y_turned, 1)
                pe.wait_ge(yb_loaded, 16 * n + 16)
                for k in range(4):
                    last = turn(bank[6][:, k * P:(k + 1) * P], yb_in[:, k * P:(k + 1) * P])
                last.then_inc(y_turned, 1)

            def project_y(p, b, k):
                n = index_a(p, b)
                if k % 4 == 0:
                    pe.wait_ge(yt_lo_set, 2 * n + 1 + k // 4)
                if k == 0:
                    ge(pe, post_set, n)
                if isinstance(n, int) and n == 0:
                    pe.wait_ge(wo_lo_set, k + 1)
                for part in range(2):
                    for half in range(2):
                        for w in (wo_hi, wo_lo)[:2 - part]:
                            last = pe.matmul(bank[3 + half][:, :], yt_a[:, part, k, :],
                                             w[:, k, half * HALF:(half + 1) * HALF],
                                             start=(k == 0 and part == 0 and w is wo_hi),
                                             stop=(k == KT - 1 and part == 1))
                if k == KT - 1:
                    last.then_inc(y_projected, 1)

            def mix(p, b):
                n = index_a(p, b)
                pe.wait_ge(vn_set, n + 1)
                for g in range(AG):
                    last = pe.matmul(bank[O_BANK][:, g * AD:(g + 1) * AD], ws_t[:, g, :],
                                     v_act[:, g * AD:(g + 1) * AD], start=True, stop=True)
                last.then_inc(mixed, 1)

            def step_a(p, b):
                now, behind = (p, b), later_a(p, b, -1)
                for k in range(KT):
                    if exists_a(*now):
                        project_a(*now, k, first=(k == 0), last_tile=(k == KT - 1))
                    if k == 1:
                        turn_y(*behind)
                for k in range(KT):
                    project_y(*behind, k)
                    if k == 4 and exists_a(*now):
                        mix(*now)

            last_b, before_last = ((NB - 1) // 2, (NB - 1) % 2), ((NB - 2) // 2, (NB - 2) % 2)
            attend(*before_last)
            pe.wait_ge(q_lo_set, NB)
            pe.wait_ge(gate_b_set, NB)
            pe.wait_ge(v_set, NB)
            for i, k in enumerate(FIRST_USED):
                pe.wait_ge(wa_lo_set, i + 1)
                project_a(0, 0, k, first=(i == 0), last_tile=(i == KT - 1))
                if i == 0:
                    turn_qk(*last_b)
                if i == 2:
                    score(*last_b)
            turn_probs(*last_b, 0)
            pe.wait_ge(ws_masked, 1)
            for k in range(KT):
                project_a(0, 1, k, first=(k == 0), last_tile=(k == KT - 1))
                if k == 1:
                    turn_probs(*last_b, 1)
                if k == 2:
                    attend(*last_b)
                if k == 4:
                    pe.wait_ge(o_read, NB)
                    mix(0, 0)
                if k == 6:
                    turn_y(0, 0)
            for k in range(KT):
                project_y(0, 0, k)
                if k == 4:
                    mix(0, 1)
            run_a(pe, step_a)

        @block.scalar
        def _(act):
            def copy(target, source, scale=1.0):
                return act.activation(target, source, ACTF.Copy, scale=scale)

            def turned_hi(p, b):
                n = index(p, b)
                act.wait_ge(xt_in[b], 16 * p + 16)
                copy(xt[:, b, 0], xt_raw[:, b, 1]).then_inc(xt_hi_set, 1)

            def square(p, b):
                n = index(p, b)
                act.wait_ge(x_in[b], 16 * p + 16)
                ge(act, x_squared, n)
                act.activation(squares, xs[:, b, :], ACTF.Square, scale=float(D) ** -0.5,
                               accum_out=mean_sq_x(b)).then_inc(x_squared, 1)

            def leave_projection(p, b):
                n = index(p, b)
                act.wait_ge(rstd_set, n + 1)
                act.wait_ge(projected, n + 1)
                copy(q_tok[:, :, 0, :].bitcast(F32R), bank[Q_BANK][:, :].rearrange("p (h d) -> p h d", h=H),
                     rstd_b(b, 1)).then_inc(q_hi_set, 1)
                for c in range(2):
                    last = copy(k_tok[:, 0, :, c, :].bitcast(F32R),
                                bank[KV_BANK][:, 0:KVW].rearrange("p (g d) -> p g d", g=G), rstd_b(b, 0))
                last.then_inc(k_hi_set, 1)
                ge(act, yb_set, n - 1)
                act.activation(gate_b[:, b, :], bank[Z_BANK][:, :], ACTF.Tanh, scale=rstd_b(b, 2)).then_inc(z_tanh_set, 1)
                ge(act, attended, n)
                act.wait_ge(k_lo_set, n + 1)
                copy(v_tok[:, b, :], bank[KV_BANK][:, KVW:2 * KVW], rstd_b(b, 0)).then_inc(v_set, 1)

            def stack(p, b):
                n = index(p, b)
                for j in range(2):
                    act.wait_ge(qk_turned, 3 * n + 1 + j)
                    copy(q_stack[:, 4 * j:4 * j + 4, :], bank[T_BANK + j][:, :]
                         .rearrange("p (h t) -> p h t", h=4)).then_inc(stacked, 1)
                act.wait_ge(qk_turned, 3 * n + 3)
                copy(k_stack[:, :, b, :], bank[T_BANK + 2][:, :].rearrange("p (j t) -> p j t", j=2 * G)).then_inc(stacked, 1)

            def exponentials(p, b, half):
                n = index(p, b)
                keys = P if isinstance(n, int) and n == 0 else 2 * P
                for h in range(4 * half, 4 * half + 4):
                    if h % 4 == 0:
                        act.wait_ge(max_set, 2 * n + 1 + h // 4)
                    act.activation(probs[:, h, 0:keys], probs[:, h, 0:keys], ACTF.Exp,
                                   bias=neg_max[:, h:h + 1], accum_out=row_sum[:, h:h + 1]).then_inc(exp_set, 1)
                if half == 1:
                    act.activation(sink_exp, sink_diff, ACTF.Exp).then_inc(sink_exp_set, 1)

            def leave_probs(p, b):
                n = index(p, b)
                used = 1 if isinstance(n, int) and n == 0 else 2
                for j in (0, 2):
                    act.wait_ge(p_turned, 4 * n + 1 + j)
                    copy(probs_t[:, 2 * j:2 * j + 2, 0:used, :],
                         bank[T_BANK + j][:, :].rearrange("p (h s t) -> p h s t", h=2, s=2)[:, :, 0:used, :]).then_inc(p_copied_act, 1)

            def split_a(i):
                k = FIRST_USED[i]
                act.wait_ge(wa_in[k], 16)
                wait_wb_used(act, hi_after(k))
                source = wa_stage if k in STAGED else wa_raw
                copy(wa_hi[:, k, :], source[:, k, :], gain[:, k:k + 1]).then_inc(wa_hi_set, 1)

            def step(p, b):
                ahead, behind = later(p, b, 1), later(p, b, -1)
                if exists(*behind):
                    leave_projection(*behind)
                if exists(*ahead):
                    square(*ahead)
                    turned_hi(*ahead)
                else:
                    turned_hi_a(0, 0)
                if exists(*behind):
                    stack(*behind)
                if not exists(*ahead):
                    for i in range(3):
                        split_a(i)
                if exists(*behind):
                    exponentials(*behind, 0)
                    exponentials(*behind, 1)
                    leave_probs(*behind)

            def turned_hi_a(p, b):
                n = index_a(p, b)
                act.wait_ge(xta_in, 16 * n + 16)
                copy(xt_of(n)[:, 0], xt_raw[:, 1 if isinstance(n, int) and n == 1 else 0, 1]).then_inc(xa_hi_set, 1)

            act.wait_ge(gain_in, 16)
            for k in range(KT):
                act.wait_ge(wb_in[k], 16)
                copy(wb_hi[:, k, :], wb_raw[:, k, :], gain[:, k:k + 1]).then_inc(wb_hi_set, 1)
                if k == 0:
                    turned_hi(0, 0)
            square(0, 0)
            run_b(act, step)

            def leave_projection_a(p, b):
                n = index_a(p, b)
                act.wait_ge(rstd_a_set, n + 1)
                act.wait_ge(a_projected, n + 1)
                ge(act, post_set, n - 1)
                act.activation(v_act, bank[1][:, :], ACTF.Gelu_apprx_tanh, scale=rstd_a(b, 0)).then_inc(v_act_set, 1)
                act.activation(gate_a, bank[2][:, :], ACTF.Tanh, scale=rstd_a(b, 1)).then_inc(za_tanh_set, 1)
                act.activation(bank[0][:, :], bank[0][:, :], ACTF.Gelu_apprx_tanh, scale=rstd_a(b, 0)).then_inc(u_act_set, 1)

            def turned_hi_y(p, b):
                n = index_a(p, b)
                for half in range(2):
                    act.wait_ge(y_turned, 2 * n + 1 + half)
                    copy(yt_a[:, 0, 4 * half:4 * half + 4, :],
                         bank[5 + half][:, :].rearrange("p (k t) -> p k t", k=4)).then_inc(yt_hi_set, 1)

            def step_a(p, b):
                now, ahead, behind = (p, b), later_a(p, b, 1), later_a(p, b, -1)
                turned_hi_y(*behind)
                if exists_a(*now):
                    leave_projection_a(*now)
                if exists_a(*ahead):
                    turned_hi_a(*ahead)

            last_b = ((NB - 1) // 2, (NB - 1) % 2)
            leave_projection(*last_b)
            split_a(3)
            stack(*last_b)
            for i in range(4, KT):
                split_a(i)
            turned_hi_a(0, 1)
            exponentials(*last_b, 0)
            leave_projection_a(0, 0)
            exponentials(*last_b, 1)
            leave_probs(*last_b)
            act.wait_ge(yb_set, NB)
            for j in range(2):
                act.wait_ge(yb_stored[j], 16 * (NB // 2))
            for k in range(KT):
                act.wait_ge(wo_in[k], 16)
                copy(wo_hi[:, k, :], wo_raw[:, k, :]).then_inc(wo_hi_set, 1)
            act.wait_ge(a_projected, 2)
            turned_hi_y(0, 0)
            leave_projection_a(0, 1)
            turned_hi_a(0, 2)
            run_a(act, step_a)

        @block.vector
        def _(dve):
            def turned_lo(p, b):
                n = index(p, b)
                dve.wait_ge(xt_hi_set, n + 1)
                dve.tensor_tensor(xt[:, b, 1], xt_raw[:, b, 1], xt[:, b, 0].bitcast(F32), ALU.subtract).then_inc(xt_lo_set, 1)

            STEPS_X = 1 + RSQRT_STEPS

            def rms_of_x(p, b):
                n = index(p, b)
                base = STEPS_X * n
                dve.wait_ge(x_squared, n + 1)
                dve.tensor_scalar(mean_sq, mean_sq_x(b), NORM_EPS, None, ALU.add).then_inc(stats_steps, 1)
                dve.wait_ge(stats_steps, base + 1)
                rsqrt(dve, stats_steps, base + 1, mean_sq, rstd_b(b, 0), newton)
                dve.tensor_scalar(rstd_b(b, 1), rstd_b(b, 0), float(HD) ** -0.5, None, ALU.mult)
                dve.tensor_scalar(rstd_b(b, 2), rstd_b(b, 0), 0.5, None, ALU.mult)
                column = rstd_all[:, n:n + 1] if isinstance(n, int) else rstd_all[:, bass.ds(n, 1)]
                dve.tensor_copy(column, rstd_b(b, 0)).then_inc(rstd_set, 1)

            def leave_projection(p, b):
                n = index(p, b)
                dve.wait_ge(q_hi_set, n + 1)
                dve.scalar_tensor_tensor(out=q_tok[:, :, 1, :].bitcast(F32R),
                                         in0=bank[Q_BANK][:, :].rearrange("p (h d) -> p h d", h=H), scalar=rstd_b(b, 1),
                                         in1=q_tok[:, :, 0, :], op0=ALU.mult, op1=ALU.subtract).then_inc(q_lo_set, 1)
                dve.wait_ge(k_hi_set, n + 1)
                for c in range(2):
                    last = dve.scalar_tensor_tensor(out=k_tok[:, 1, :, c, :].bitcast(F32R),
                                                    in0=bank[KV_BANK][:, 0:KVW].rearrange("p (g d) -> p g d", g=G),
                                                    scalar=rstd_b(b, 0), in1=k_tok[:, 0, :, 0, :],
                                                    op0=ALU.mult, op1=ALU.subtract)
                last.then_inc(k_lo_set, 1)
                dve.wait_ge(z_tanh_set, n + 1)
                dve.tensor_scalar(gate_b[:, b, :], gate_b[:, b, :], 1.0, rstd_b(b, 2), ALU.add, ALU.mult).then_inc(gate_steps, 1)
                dve.wait_ge(gate_steps, n + 1)
                dve.tensor_tensor(gate_b[:, b, :], bank[Z_BANK][:, :], gate_b[:, b, :], ALU.mult).then_inc(gate_b_set, 1)

            STEPS_S = 5

            def soft_max(p, b):
                n = index(p, b)
                base = STEPS_S * n
                keys = P if isinstance(n, int) and n == 0 else 2 * P
                at = P if b == 0 else 0
                for half in range(2):
                    part = slice(4 * half, 4 * half + 4)
                    for j in range(2 * half, 2 * half + 2):
                        dve.wait_ge(scored, 4 * n + j + 1)
                        last = dve.tensor_tensor(probs[:, 2 * j:2 * j + 2, 0:keys],
                                                 bank[T_BANK + j][:, :].rearrange("p (h k) -> p h k", h=2)[:, :, 0:keys],
                                                 bias[:, 2 * j:2 * j + 2, at:at + keys], ALU.add)
                    last.then_inc(softmax_steps, 1)
                    dve.wait_ge(softmax_steps, base + 2 * half + 1)
                    dve.tensor_reduce(row_max[:, part], probs[:, part, 0:keys], mybir.AxisListType.X, ALU.max).then_inc(softmax_steps, 1)
                    dve.wait_ge(softmax_steps, base + 2 * half + 2)
                    negated = dve.scalar_tensor_tensor(out=neg_max[:, part], in0=row_max[:, part], scalar=-1.0,
                                                       in1=neg_sink[:, part], op0=ALU.mult, op1=ALU.min)
                    negated.then_inc(softmax_steps if half else max_set, 1)
                dve.wait_ge(softmax_steps, base + 5)
                dve.tensor_tensor(sink_diff, neg_max, neg_sink[:, :], ALU.subtract).then_inc(max_set, 1)

            def leave_probs(p, b, j):
                n = index(p, b)
                used = 1 if isinstance(n, int) and n == 0 else 2
                dve.wait_ge(p_turned, 4 * n + 1 + j)
                dve.tensor_copy(probs_t[:, 2 * j:2 * j + 2, 0:used, :],
                                bank[T_BANK + j][:, :].rearrange("p (h s t) -> p h s t", h=2, s=2)[:, :, 0:used, :]).then_inc(p_copied_dve, 1)

            def denominators(p, b):
                n = index(p, b)
                dve.wait_ge(sink_exp_set, n + 1)
                dve.tensor_tensor(row_sum, row_sum, sink_exp, ALU.add).then_inc(denominator_steps, 1)
                dve.wait_ge(denominator_steps, 2 * n + 1)
                dve.reciprocal(row_inv, row_sum).then_inc(denominator_steps, 1)
                dve.wait_ge(denominator_steps, 2 * n + 2)

            def gate(p, b):
                n = index(p, b)
                dve.wait_ge(attended, n + 1)
                ge(dve, yb_stored[b], 16 * p)
                dve.tensor_tensor(y_b[:, b, :].rearrange("p (h d) -> p h d", h=H),
                                  bank[O_BANK][:, :].rearrange("p (h d) -> p h d", h=H),
                                  row_inv.unsqueeze(2).to_broadcast([P, H, HD]), ALU.mult).then_inc(o_read, 1)
                dve.wait_ge(o_read, n + 1)
                dve.tensor_tensor(y_b[:, b, :], y_b[:, b, :], gate_b[:, b, :], ALU.mult).then_inc(yb_set, 1)

            def split_a(i):
                k = FIRST_USED[i]
                dve.wait_ge(wa_hi_set, i + 1)
                wait_wb_used(dve, lo_after(k))
                source = wa_stage if k in STAGED else wa_raw
                dve.scalar_tensor_tensor(out=wa_lo[:, k, :], in0=source[:, k, :], scalar=gain[:, k:k + 1],
                                         in1=wa_hi[:, k, :].bitcast(F32), op0=ALU.mult, op1=ALU.subtract).then_inc(wa_lo_set, 1)

            def turned_lo_a(p, b):
                n = index_a(p, b)
                dve.wait_ge(xa_hi_set, n + 1)
                raw = xt_raw[:, 1 if isinstance(n, int) and n == 1 else 0, 1]
                dve.tensor_tensor(xt_of(n)[:, 1], raw, xt_of(n)[:, 0].bitcast(F32), ALU.subtract).then_inc(xa_lo_set, 1)

            def step(p, b):
                ahead, behind, last = later(p, b, 1), later(p, b, -1), later(p, b, -2)
                if exists(*behind):
                    leave_projection(*behind)
                if exists(*last):
                    gate(*last)
                if exists(*ahead):
                    rms_of_x(*ahead)
                    turned_lo(*ahead)
                else:
                    turned_lo_a(0, 0)
                if exists(*behind):
                    soft_max(*behind)
                    if not exists(*ahead):
                        split_a(0)
                    leave_probs(*behind, 1)
                    leave_probs(*behind, 3)
                    denominators(*behind)

            dve.wait_ge(buckets_in, 16 * 2)
            for h in range(H):
                dve.tensor_scalar(rel_rows[:, h, :], onehot, rel[:, h:h + 1], None, ALU.mult).then_inc(rel_spread, 1)
            dve.wait_ge(rel_summed, 2)
            dve.wait_ge(rows_set, 1)
            dve.tensor_copy(bias_rows[:, 0:4, P:2 * P], bank[5][:, :].rearrange("p (h j) -> p h j", h=4))
            dve.tensor_copy(bias_rows[:, 4:8, P:2 * P], bank[6][:, :].rearrange("p (h j) -> p h j", h=4)).then_inc(rows_set, 1)
            dve.wait_ge(gain_in, 16)
            for k in range(KT):
                dve.wait_ge(wb_hi_set, k + 1)
                dve.scalar_tensor_tensor(out=wb_lo[:, k, :], in0=wb_raw[:, k, :], scalar=gain[:, k:k + 1],
                                         in1=wb_hi[:, k, :].bitcast(F32), op0=ALU.mult, op1=ALU.subtract).then_inc(wb_lo_set, 1)
                if k == 0:
                    turned_lo(0, 0)
            rms_of_x(0, 0)
            dve.wait_ge(consts_in, 16 * 5)
            dve.tensor_scalar(neg_sink[:, :], neg_sink[:, :], -1.0, None, ALU.mult).then_inc(sink_negated, 1)
            dve.wait_ge(sink_negated, 1)
            dve.wait_ge(bias_in, 32)
            run_b(dve, step)

            def rstd_of_pass_b(p, b):
                n = index_a(p, b)
                column = rstd_all[:, n:n + 1] if isinstance(n, int) else rstd_all[:, bass.ds(n, 1)]
                dve.tensor_copy(rstd_a(b, 0), column).then_inc(rstd_a_steps, 1)
                dve.wait_ge(rstd_a_steps, n + 1)
                dve.tensor_scalar(rstd_a(b, 1), rstd_a(b, 0), 0.5, None, ALU.mult).then_inc(rstd_a_set, 1)

            STEPS_LN = 5 + RSQRT_STEPS

            def layer_norm(p, b):
                n = index_a(p, b)
                base = STEPS_LN * n
                done = 0

                def link(ins, then_aggregate=False):
                    nonlocal done
                    done += 1
                    ins.then_inc(ln_steps, 1)
                    dve.wait_ge(ln_steps, base + done)
                    if then_aggregate:
                        dve.memset(newton, 0.0)

                dve.wait_ge(v_act_set, n + 1)
                link(dve.bn_stats(stats[:, 0, :], v_act), then_aggregate=True)
                link(dve.bn_aggr(mean_var, stats[:, 0:1, :]))
                link(dve.tensor_scalar(mean_sq, mean_var[:, 1:2], NORM_EPS, None, ALU.add))
                rsqrt(dve, ln_steps, base + done, mean_sq, rstd_ln, newton)
                done += RSQRT_STEPS
                link(dve.tensor_scalar(v_act, v_act, mean_var[:, 0:1], rstd_ln, ALU.subtract, ALU.mult))
                link(dve.tensor_tensor(v_act, v_act, ln_gain[:, :], ALU.mult))
                dve.tensor_tensor(v_act, v_act, ln_bias[:, :], ALU.add).then_inc(vn_set, 1)
                assert done == STEPS_LN

            def gate_of_a(p, b):
                n = index_a(p, b)
                dve.wait_ge(za_tanh_set, n + 1)
                dve.tensor_scalar(gate_a, gate_a, 1.0, rstd_a(b, 1), ALU.add, ALU.mult).then_inc(gate_a_steps, 1)
                dve.wait_ge(gate_a_steps, n + 1)
                dve.tensor_tensor(gate_a, bank[2][:, :], gate_a, ALU.mult).then_inc(z_read, 1)
                dve.wait_ge(z_read, n + 1)
                dve.wait_ge(u_act_set, n + 1)
                dve.tensor_tensor(gate_a, bank[0][:, :], gate_a, ALU.mult).then_inc(u_read, 1)

            def gate_mixed(p, b):
                n = index_a(p, b)
                dve.wait_ge(mixed, n + 1)
                dve.tensor_tensor(v_act.rearrange("p (g d) -> p g d", g=AG),
                                  bank[O_BANK][:, :].rearrange("p (g d) -> p g d", g=AG),
                                  bs_t[:, :].unsqueeze(2).to_broadcast([P, AG, AD]), ALU.add).then_inc(ya_steps, 1)
                dve.wait_ge(ya_steps, n + 1)
                dve.wait_ge(u_read, n + 1)
                dve.tensor_tensor(gate_a, gate_a, v_act, ALU.mult).then_inc(ya_set, 1)
                dve.wait_ge(ya_set, n + 1)

            def turned_lo_y(p, b):
                n = index_a(p, b)
                for half in range(2):
                    dve.wait_ge(yt_hi_set, 2 * n + 1 + half)
                    dve.tensor_tensor(yt_a[:, 1, 4 * half:4 * half + 4, :],
                                      bank[5 + half][:, :].rearrange("p (k t) -> p k t", k=4),
                                      yt_a[:, 0, 4 * half:4 * half + 4, :].bitcast(F32), ALU.subtract).then_inc(yt_lo_set, 1)

            STEPS_POST = 7 + RSQRT_STEPS

            def post_norm(p, b):
                n = index_a(p, b)
                base = STEPS_POST * n
                done = 0

                def link(ins, then_aggregate=False):
                    nonlocal done
                    done += 1
                    ins.then_inc(post_steps, 1)
                    dve.wait_ge(post_steps, base + done)
                    if then_aggregate:
                        dve.memset(newton, 0.0)

                dve.wait_ge(xa_in[b], 16 * p + 16)
                dve.wait_ge(y_projected, n + 1)
                dve.bn_stats(stats[:, 0, :], bank[3][:, :])
                link(dve.bn_stats(stats[:, 1, :], bank[4][:, :]), then_aggregate=True)
                link(dve.bn_aggr(mean_var, stats[:, :, :]))
                link(dve.scalar_tensor_tensor(out=mean_sq, in0=mean_var[:, 0:1], scalar=mean_var[:, 0:1],
                                              in1=mean_var[:, 1:2], op0=ALU.mult, op1=ALU.add))
                link(dve.tensor_scalar(mean_sq, mean_sq, NORM_EPS, None, ALU.add))
                rsqrt(dve, post_steps, base + done, mean_sq, rstd_post, newton)
                done += RSQRT_STEPS
                for half in range(2):
                    part = slice(half * HALF, (half + 1) * HALF)
                    link(dve.scalar_tensor_tensor(out=v_act, in0=bank[3 + half][:, :], scalar=rstd_post,
                                                  in1=post_gain[:, part], op0=ALU.mult, op1=ALU.mult))
                    last = dve.tensor_tensor(xs[:, b, part], xs[:, b, part], v_act, ALU.add)
                    if half == 0:
                        link(last)
                last.then_inc(post_set, 1)
                assert done == STEPS_POST

            def step_a(p, b):
                now, ahead, behind = (p, b), later_a(p, b, 1), later_a(p, b, -1)
                turned_lo_y(*behind)
                if exists_a(*now):
                    layer_norm(*now)
                    gate_of_a(*now)
                if exists_a(*ahead):
                    turned_lo_a(*ahead)
                    rstd_of_pass_b(*ahead)
                if exists_a(*now):
                    gate_mixed(*now)
                post_norm(*behind)

            last_b, before_last = ((NB - 1) // 2, (NB - 1) % 2), ((NB - 2) // 2, (NB - 2) % 2)
            rstd_of_pass_b(0, 0)
            leave_projection(*last_b)
            split_a(1)
            split_a(2)
            gate(*before_last)
            for i in range(3, KT):
                split_a(i)
            turned_lo_a(0, 1)
            soft_max(*last_b)
            gate_of_a(0, 0)
            rstd_of_pass_b(0, 1)
            leave_probs(*last_b, 1)
            leave_probs(*last_b, 3)
            denominators(*last_b)
            layer_norm(0, 0)
            gate(*last_b)
            gate_mixed(0, 0)
            for k in range(KT):
                dve.wait_ge(wo_hi_set, k + 1)
                dve.tensor_tensor(wo_lo[:, k, :], wo_raw[:, k, :], wo_hi[:, k, :].bitcast(F32), ALU.subtract).then_inc(wo_lo_set, 1)
            turned_lo_y(0, 0)
            layer_norm(0, 1)
            gate_of_a(0, 1)
            turned_lo_a(0, 2)
            rstd_of_pass_b(0, 2)
            gate_mixed(0, 1)
            post_norm(0, 0)
            run_a(dve, step_a)


def kernel(x, pre_norm_g, w_in, ln_v_g, ln_v_b, w_spatial, b_spatial, sinks, rel_bias, w_out, post_norm_g):
    import concourse.bacc as bacc
    from concourse.bass_utils import run_bass_kernel_spmd

    buckets = rel_bias.shape[0]
    distance = np.arange(P - 1, -1, -1)
    exact = buckets // 2
    far = exact + (np.log(np.maximum(distance, 1) / exact) / math.log(REL_MAX_DIST / exact) * (buckets - exact)).astype(np.int32)
    bucket = np.where(distance < exact, distance, np.minimum(far, buckets - 1))
    onehot = np.equal(np.arange(buckets)[:, None], bucket[None, :]).astype(np.float32)

    arrays = {
        "x": x, "x_turned": x[0].reshape(-1, P, x.shape[2] // P, P).transpose(0, 3, 2, 1), "pre_norm_g": pre_norm_g.reshape(-1, P).T, "w_in": w_in, "ln_v_g": ln_v_g, "ln_v_b": ln_v_b,
        "w_spatial": w_spatial[0].transpose(2, 0, 1), "b_spatial": b_spatial[0].T, "sinks": sinks, "rel_bias": rel_bias,
        "w_out": w_out, "post_norm_g": post_norm_g, "bucket_onehot": onehot, "identity": np.eye(P, dtype=np.float32),
    }
    arrays = {f"in_{name}": np.ascontiguousarray(a) for name, a in arrays.items()}
    nc = bacc.Bacc("TRN2", target_bir_lowering=False, num_devices=1)
    args = [nc.dram_tensor(name, a.shape, mybir.dt.from_np(a.dtype), kind="ExternalInput").ap() for name, a in arrays.items()]
    out = nc.dram_tensor("out", x.shape, F32, kind="ExternalOutput").ap()
    build(nc, *args, out)
    result = run_bass_kernel_spmd(nc, [arrays], core_ids=[0])
    return result.results[0]["out"]
```

```python
from contextlib import ExitStack
import math

import numpy as np
import concourse.bass as bass
from concourse import mybir

F32 = mybir.dt.float32
F32R = mybir.dt.float32r
I32 = mybir.dt.int32
ALU = mybir.AluOpType
ACTF = mybir.ActivationFunctionType

P = 128
MASKED = -1e30
NORM_EPS = 1e-6
REL_MAX_DIST = 128
STATS = 6
HALF = 512
RSQRT_STEPS = 10
X_SLOTS = 2


def ge(eng, sem, value):
    if isinstance(value, int) and value <= 0:
        return
    eng.wait_ge(sem, value)


def rsqrt(dve, sem, base, x, y, tmp):
    done = 0

    def link(ins):
        nonlocal done
        done += 1
        ins.then_inc(sem, 1)
        dve.wait_ge(sem, base + done)

    link(dve.tensor_scalar(y.bitcast(I32), x.bitcast(I32), -0.5, 1597463007.0, ALU.mult, ALU.add))
    for _ in range(3):
        link(dve.scalar_tensor_tensor(out=tmp, in0=y, scalar=y, in1=x, op0=ALU.mult, op1=ALU.mult))
        link(dve.tensor_scalar(tmp, tmp, -0.5, 1.5, ALU.mult, ALU.add))
        link(dve.tensor_tensor(y, y, tmp, ALU.mult))
    assert done == RSQRT_STEPS


def build(nc, x, x_t, pre_g, w_in, ln_g, ln_b, w_spatial, b_spatial, sinks, rel_bias, w_out, post_g,
          bucket_onehot, identity, out):
    _, SEQ, D = x.shape
    AW = ln_g.shape[1]
    AG = w_spatial.shape[1]
    AD = AW // AG
    H = sinks.shape[1]
    BUCKETS = rel_bias.shape[0]
    HD = (w_out.shape[1] - AW) // H
    BW = H * HD
    KVW = (w_in.shape[2] - 3 * AW - 2 * BW) // 2
    G = KVW // HD
    GH = H // G
    NB = SEQ // P
    KT = D // P
    BCOLS = 2 * BW + 2 * KVW
    ACOLS = 3 * AW
    assert D == 2 * HALF and AW == HALF and BW == HALF and HD == 64 and H == 8 and G == 2 and NB == 32

    y_scratch = nc.dram_tensor("y_b_scratch", [NB, P, BW], F32, kind="Internal").ap()
    PITCH = 3 * P
    bias_scratch = nc.dram_tensor("bias_scratch", [H, P, PITCH], F32, kind="Internal")

    x_blocks = x.rearrange("o (n p) d -> (o n) p d", p=P)
    out_blocks = out.rearrange("o (n p) d -> (o n) p d", p=P)

    ctx = ExitStack()
    with ctx:
        def sb(stack, name, shape, dt=F32):
            return stack.enter_context(nc.sbuf_tensor(name, shape, dt))

        ident = sb(ctx, "ident", [P, P])
        post_gain = sb(ctx, "post_gain", [P, D])
        ln_gain = sb(ctx, "ln_gain", [P, AW])
        ln_bias = sb(ctx, "ln_bias", [P, AW])
        ws_t = sb(ctx, "ws_t", [P, AG, P])
        bs_t = sb(ctx, "bs_t", [P, AG])
        gain = sb(ctx, "gain", [P, KT])
        neg_sink = sb(ctx, "neg_sink", [P, H])
        rstd_all = sb(ctx, "rstd_all", [P, NB])
        small = sb(ctx, "small", [P, 32])
        stats = sb(ctx, "stats", [P, 2, STATS])
        xs = sb(ctx, "xs", [P, X_SLOTS, D])
        act_buf = sb(ctx, "act_buf", [P, 5, HALF])
        over = ExitStack()
        xt_raw = sb(over, "xt_raw", [P, 2, 2, KT, P])
        over.close()
        xt = sb(ctx, "xt", [P, 2, 2, KT, P], F32R)

        over = ExitStack()
        wb_hi = sb(over, "wb_hi", [P, KT, BCOLS], F32R)
        wb_lo = sb(over, "wb_lo", [P, KT, BCOLS], F32R)
        over.close()
        over = ExitStack()
        sb(over, "under_wb_raw", [P, KT, BCOLS])
        wb_raw = sb(over, "wb_raw", [P, KT, BCOLS])
        over.close()
        over = ExitStack()
        sb(over, "under_wa_raw", [P, KT, ACOLS])
        wa_raw = sb(over, "wa_raw", [P, KT, ACOLS])
        over.close()
        wa_hi = sb(ctx, "wa_hi", [P, KT, ACOLS], F32R)
        wa_lo = sb(ctx, "wa_lo", [P, KT, ACOLS], F32R)

        work = ExitStack()
        probs = sb(work, "probs", [P, H, 2 * P])
        probs_t = sb(work, "probs_t", [P, H, 2, P])
        k_stack = sb(work, "k_stack", [P, 2 * G, 2, P], F32R)
        y_b = sb(work, "y_b", [P, 2, BW])
        gate_b = sb(work, "gate_b", [P, 2, BW])
        k_tok = sb(work, "k_tok", [P, 2, KVW])
        v_tok = sb(work, "v_tok", [P, 2, KVW])
        row = sb(work, "row", [P, 6, H])
        own_keys = sb(work, "own_keys", [P, P])
        filled = 4 * H * P + 2 * G * 2 * P + 4 * BW + 4 * KVW + 6 * H + P
        assert filled <= KT * D
        if filled < KT * D:
            sb(work, "pad", [P, KT * D - filled])
        wa_stage = sb(work, "wa_stage", [P, 2, ACOLS])
        q_tok = sb(work, "q_tok", [P, 2, BW])
        q_stack = sb(work, "q_stack", [P, H, P], F32R)
        bias = sb(work, "bias", [P, H, 3 * P])
        work.close()
        assert 2 * D == H * 2 * P and D == 2 * G * 2 * P == H * P == 2 * BW and 3 * D == 2 * ACOLS == H * 3 * P
        over = ExitStack()
        sb(over, "under_wo_raw", [P, KT, D])
        wo_raw = sb(over, "wo_raw", [P, KT, D])
        over.close()
        wo_hi = sb(ctx, "wo_hi", [P, KT, D], F32R)
        wo_lo = sb(ctx, "wo_lo", [P, KT, D], F32R)

        row_max, neg_max, sink_diff, row_sum, sink_exp, row_inv = (row[:, j, :] for j in range(6))
        mean_var = small[:, 0:2]
        mean_sq, newton = small[:, 2:3], small[:, 3:4]
        rstd_ln, rstd_post = small[:, 4:5], small[:, 5:6]

        def mean_sq_x(slot):
            return small[:, 20 + slot:21 + slot]

        def rstd_b(slot, j):
            return small[:, 8 + 3 * slot + j:9 + 3 * slot + j]

        def rstd_a(slot, j):
            return small[:, 16 + 2 * slot + j:17 + 2 * slot + j]

        v_act = (act_buf[:, 0, :], act_buf[:, 1, :])
        gate_a = (act_buf[:, 2, :], act_buf[:, 3, :])
        yb_in = act_buf[:, 4, :]
        squares = act_buf[:, 0:2, :].rearrange("p a b -> p (a b)")
        rel_rows = probs[0:BUCKETS, 0:4, :].rearrange("p h (c j) -> p (h c) j", c=2)
        onehot = probs_t[0:BUCKETS, 0, 0, :]
        ones = probs_t[0:BUCKETS, 0, 1, :]
        rel = probs_t[0:BUCKETS, 1, 0, 0:H]
        bias_rows = wa_stage[:, :, :].rearrange("p a b -> p (a b)").rearrange("p (h j) -> p h j", h=H)

        bank = [ctx.enter_context(nc.psum_tensor(f"bank{j}", [P, HALF], F32)) for j in range(8)]
        Q_BANK, KV_BANK, Z_BANK, T_BANK, O_BANK = 0, 1, 2, 3, 7

        def sem(name):
            return ctx.enter_context(nc.semaphore(name))

        ident_in, gain_in, consts_in, sinks_in, ws_in, buckets_in, bias_out, bias_in = (sem(s) for s in (
            "ident_in", "gain_in", "consts_in", "sinks_in", "ws_in", "buckets_in", "bias_out", "bias_in"))
        ones_set, rel_spread, rel_summed, rows_set, sink_negated = (sem(s) for s in (
            "ones_set", "rel_spread", "rel_summed", "rows_set", "sink_negated"))
        ws_masked, own_keys_set = sem("ws_masked"), sem("own_keys_set")
        wb_in = [sem(f"wb_in{k}") for k in range(KT)]
        wa_in = [sem(f"wa_in{k}") for k in range(KT)]
        wo_in = [sem(f"wo_in{k}") for k in range(KT)]
        wb_used = sem("wb_used")
        wb_hi_set, wb_lo_set, wa_hi_set, wa_lo_set, wo_hi_set, wo_lo_set = (sem(s) for s in (
            "wb_hi_set", "wb_lo_set", "wa_hi_set", "wa_lo_set", "wo_hi_set", "wo_lo_set"))
        x_in = [sem(f"x_in{j}") for j in range(2)]
        xt_in = [sem(f"xt_in{j}") for j in range(2)]
        xt_hi_set, xt_lo_set, x_squared, rstd_set = (sem(s) for s in (
            "xt_hi_set", "xt_lo_set", "x_squared", "rstd_set"))
        projected, q_copied, k_copied, v_set, z_tanh_set, gate_b_set, stack_hi_set = (sem(s) for s in (
            "projected", "q_copied", "k_copied", "v_set", "z_tanh_set", "gate_b_set", "stack_hi_set"))
        qk_turned, stacked, scored, max_set, exp_set, sink_exp_set = (sem(s) for s in (
            "qk_turned", "stacked", "scored", "max_set", "exp_set", "sink_exp_set"))
        p_turned, p_parted, p_copied, attended, o_read, yb_set = (sem(s) for s in (
            "p_turned", "p_parted", "p_copied", "attended", "o_read", "yb_set"))
        yb_stored = [sem(f"yb_stored{j}") for j in range(2)]
        stats_steps, softmax_steps, gate_steps, denominator_steps = (sem(s) for s in (
            "stats_steps", "softmax_steps", "gate_steps", "denominator_steps"))
        xa_in = [sem(f"xa_in{j}") for j in range(X_SLOTS)]
        yb_loaded = sem("yb_loaded")
        xta_in, xa_hi_set, xa_lo_set, rstd_a_set = (sem(s) for s in (
            "xta_in", "xa_hi_set", "xa_lo_set", "rstd_a_set"))
        a_projected, v_act_set, za_tanh_set, u_act_set, z_read, u_read, vn_set = (sem(s) for s in (
            "a_projected", "v_act_set", "za_tanh_set", "u_act_set", "z_read", "u_read", "vn_set"))
        mixed, mix_read, ya_set, y_turned, yt_hi_set, yt_lo_set, y_projected, post_set = (sem(s) for s in (
            "mixed", "mix_read", "ya_set", "y_turned", "yt_hi_set", "yt_lo_set", "y_projected", "post_set"))
        out_stored = [sem(f"out_stored{j}") for j in range(X_SLOTS)]
        ln_steps, gate_a_steps, post_steps, rstd_a_steps = (sem(s) for s in (
            "ln_steps", "gate_a_steps", "post_steps", "rstd_a_steps"))

        def later(p, b, d):
            return p + (b + d) // 2, (b + d) % 2

        def index(p, b):
            return 2 * p + b

        def exists(p, b):
            n = index(p, b)
            return not isinstance(n, int) or 0 <= n < NB

        def run_b(eng, step):
            for s in range(3):
                step(s // 2, s % 2)
            with eng.Fori(0, (NB - 4) // 2) as i:
                step(i + 1, 1)
                step(i + 2, 0)
            step((NB - 1) // 2, (NB - 1) % 2)

        def run_a(eng, step):
            with eng.Fori(1, NB // 2 - 1) as i:
                step(i, 1)
                step(i + 1, 0)
            step((NB - 1) // 2, (NB - 1) % 2)

        def y_banks(n):
            if isinstance(n, int) and n >= NB - 2:
                return (0, 1) if n == NB - 2 else (6, 7)
            return (3, 4)

        def yt_of(n):
            return xt[:, 0] if isinstance(n, int) and n == NB - 2 else xt[:, 1]

        def xt_of(n):
            return xt[:, 1] if isinstance(n, int) and n == 1 else xt[:, 0]

        def row_of(blocks, n):
            if isinstance(n, int):
                return blocks[n]
            return blocks[bass.ds(n, 1)].rearrange("n p d -> p (n d)")

        block = ctx.enter_context(nc.Block())

        w_rows = w_in[0].rearrange("(k p) c -> k p c", p=P)
        wo_rows = w_out[0].rearrange("(k p) c -> k p c", p=P)
        def reach(last_value, first_tile):
            return min(KT, -(-(last_value - first_tile * BCOLS) // BCOLS))

        def hi_after(k):
            end = (k + 1) * ACOLS
            if k * ACOLS >= KT * BCOLS:
                return reach(end, KT)
            return KT if end > KT * BCOLS else reach(end, 0)

        def lo_after(k):
            if (KT + k) * ACOLS >= 2 * KT * BCOLS:
                return 0
            return reach((KT + k + 1) * ACOLS, KT)

        BESIDE = [k for k in range(KT) if lo_after(k) == 0]
        FIRST_USED = [0, KT - 1, 1] + [k for k in range(2, KT - 1) if k in BESIDE] + [
            k for k in range(2, KT - 1) if k not in BESIDE]
        STAGED = (0, 1)

        def wait_wb_used(eng, tiles):
            if tiles == KT:
                eng.wait_ge(projected, NB)
            elif tiles > 0:
                eng.wait_ge(wb_used, tiles)

        def row_of_t(n):
            if isinstance(n, int):
                return x_t[n]
            return x_t[bass.ds(n, 1)].rearrange("n p k t -> p (n k) t")

        @block.sync
        def _(sp):
            sp.dma_start(onehot, bucket_onehot).then_inc(buckets_in, 16)
            sp.dma_start(rel, rel_bias).then_inc(buckets_in, 16)
            sp.dma_start(gain[:, :], pre_g).then_inc(gain_in, 16)
            for k in range(KT):
                if k == 0:
                    sp.dma_start(xt_raw[:, 0, 1], row_of_t(0)).then_inc(xt_in[0], 16)
                if k == KT - 2:
                    sp.dma_start(xs[:, 0, :], x_blocks[0]).then_inc(x_in[0], 16)
                if k == KT - 1:
                    sp.dma_start(xt_raw[:, 1, 1], row_of_t(1)).then_inc(xt_in[1], 16)
                sp.dma_start(wb_raw[:, k, :], w_rows[k, :, ACOLS:]).then_inc(wb_in[k], 16)
            sp.dma_start(ident[:, :], identity).then_inc(ident_in, 16)
            sp.dma_start(xs[:, 1, :], x_blocks[1]).then_inc(x_in[1], 16)

            def step(p, b):
                pp, slot = later(p, b, 1)
                if exists(pp, slot) and exists(*later(p, b, -1)):
                    n = index(p, b)
                    sp.wait_ge(projected, n)
                    sp.dma_start(xt_raw[:, slot, 1], row_of_t(n + 1)).then_inc(xt_in[slot], 16)
                    sp.wait_ge(x_squared, n)
                    sp.dma_start(xs[:, slot, :], row_of(x_blocks, n + 1)).then_inc(x_in[slot], 16)
                if exists(*later(p, b, -2)):
                    n = index(p, b) - 2
                    sp.wait_ge(yb_set, n + 1)
                    sp.dma_start(row_of(y_scratch, n), y_b[:, b, :]).then_inc(yb_stored[b], 16)

            def step_b(p, b):
                s = index(p, b)
                if isinstance(s, int) and s == NB - 1:
                    sp.wait_ge(projected, NB - 1)
                    sp.dma_start(xt_raw[:, 0, 1], row_of_t(0)).then_inc(xta_in, 16)
                    sp.wait_ge(bias_out, 16)
                    for k in STAGED:
                        sp.dma_start(wa_stage[:, k, :], w_rows[k, :, 0:ACOLS]).then_inc(wa_in[k], 16)
                    for k in BESIDE:
                        sp.dma_start(wa_raw[:, k, :], w_rows[k, :, 0:ACOLS]).then_inc(wa_in[k], 16)
                step(p, b)

            run_b(sp, step_b)
            for k in range(KT):
                if k not in BESIDE and k not in STAGED:
                    wait_wb_used(sp, lo_after(k))
                    sp.dma_start(wa_raw[:, k, :], w_rows[k, :, 0:ACOLS]).then_inc(wa_in[k], 16)
            sp.wait_ge(projected, NB)
            sp.wait_ge(xta_in, 16)
            sp.dma_start(xt_raw[:, 1, 1], row_of_t(1)).then_inc(xta_in, 16)
            sp.wait_ge(x_squared, NB)
            for j in range(2):
                sp.dma_start(xs[:, j, :], x_blocks[j]).then_inc(xa_in[j], 16)
            sp.wait_ge(yb_set, NB - 1)
            sp.dma_start(y_scratch[NB - 2], y_b[:, 0, :]).then_inc(yb_stored[0], 16)
            sp.wait_ge(yb_stored[0], 16 * (NB // 2))
            sp.dma_start(yb_in, y_scratch[0]).then_inc(yb_loaded, 16)
            sp.wait_ge(scored, 4 * NB)
            sp.wait_ge(wa_lo_set, 3)
            for k in range(KT):
                if k == KT - 3:
                    sp.wait_ge(max_set, 2 * NB)
                sp.dma_start(wo_raw[:, k, :], wo_rows[k]).then_inc(wo_in[k], 16)
            sp.wait_ge(a_projected, 1)
            sp.wait_ge(xta_in, 32)
            sp.dma_start(xt_raw[:, 0, 1], row_of_t(2)).then_inc(xta_in, 16)
            sp.wait_ge(yb_set, NB)
            sp.dma_start(y_scratch[NB - 1], y_b[:, 1, :]).then_inc(yb_stored[1], 16)
            sp.wait_ge(yb_stored[1], 16 * (NB // 2))

            def step_a(p, b):
                n = index(p, b)
                sp.wait_ge(y_turned, 2 * (n - 1))
                sp.dma_start(yb_in, row_of(y_scratch, n - 1)).then_inc(yb_loaded, 16)
                if exists(*later(p, b, 1)):
                    sp.wait_ge(a_projected, n + 1)
                    sp.dma_start(xt_raw[:, 0, 1], row_of_t(n + 1)).then_inc(xta_in, 16)
                else:
                    sp.wait_ge(y_turned, 2 * n)
                    sp.dma_start(yb_in, y_scratch[n]).then_inc(yb_loaded, 16)
                sp.wait_ge(post_set, n - 1)
                sp.dma_start(row_of(out_blocks, n - 2), xs[:, b, :]).then_inc(out_stored[b], 16)
                sp.wait_ge(out_stored[b], 16 * p)
                sp.dma_start(xs[:, b, :], row_of(x_blocks, n)).then_inc(xa_in[b], 16)

            step_a(1, 0)
            run_a(sp, step_a)
            for n in (NB - 2, NB - 1):
                sp.wait_ge(post_set, n + 1)
                sp.dma_start(out_blocks[n], xs[:, n % 2, :]).then_inc(out_stored[n % 2], 16)
            for j in range(2):
                sp.wait_ge(out_stored[j], 16 * (NB // 2))

        @block.gpsimd
        def _(pool):
            pool.memset(ones, 1.0).then_inc(ones_set, 1)
            pool.memset(bias_rows, MASKED).then_inc(rows_set, 1)
            pool.memset(own_keys[:, :], 1.0).then_inc(own_keys_set, 1)
            pool.wait_ge(own_keys_set, 1)
            pool.affine_select(out=own_keys[:, :], in_=own_keys[:, :], compare_op=ALU.is_ge, fill=0.0, base=0,
                               pattern=[[1, P]], channel_multiplier=-1).then_inc(own_keys_set, 1)
            pool.dma_start(neg_sink[:, :], sinks[0].partition_broadcast(P)).then_inc(sinks_in, 16)
            pool.wait_ge(wb_in[KT - 1], 16)
            pool.wait_ge(rows_set, 2)
            pool.dma_start(bias_scratch.ap().rearrange("h p j -> p h j"), bias_rows).then_inc(bias_out, 16)
            pool.wait_ge(bias_out, 16)
            for at, keys in ((0, 2 * P), (2 * P, P)):
                pool.dma_start(bias[:, :, at:at + keys],
                               bass.AP(bias_scratch, P - 1, [[PITCH - 1, P], [P * PITCH, H], [1, keys]])).then_inc(bias_in, 16)
            pool.dma_start(ws_t[:, :, :], w_spatial).then_inc(ws_in, 16)
            for target, source in ((post_gain, post_g[0]), (ln_gain, ln_g[0]), (ln_bias, ln_b[0])):
                pool.dma_start(target[:, :], source.partition_broadcast(P)).then_inc(consts_in, 16)
            pool.dma_start(bs_t[:, :], b_spatial).then_inc(consts_in, 16)
            pool.wait_ge(ws_in, 16)
            pool.affine_select(out=ws_t[:, :, :], in_=ws_t[:, :, :], compare_op=ALU.is_ge, fill=0.0, base=0,
                               pattern=[[0, AG], [1, P]], channel_multiplier=-1).then_inc(ws_masked, 1)

        @block.tensor
        def _(pe):
            def turn(target, source):
                return pe.transpose(target, source, ident[:, :])

            def project_k(p, b, k):
                n = index(p, b)
                if k == 0:
                    pe.wait_ge(xt_lo_set, n + 1)
                if isinstance(n, int) and n == 0:
                    pe.wait_ge(wb_lo_set, k + 1)
                cols = ((Q_BANK, 0, BW, q_copied), (Z_BANK, BW + 2 * KVW, BCOLS, gate_b_set),
                        (KV_BANK, BW, BW + 2 * KVW, v_set))
                for part in range(2):
                    for j, a, e, emptied in cols:
                        if k == 0 and part == 0:
                            ge(pe, emptied, n)
                        for w in (wb_hi, wb_lo)[:2 - part]:
                            last = pe.matmul(bank[j][:, 0:e - a], xt[:, b, part, k, :], w[:, k, a:e],
                                             start=(k == 0 and part == 0 and w is wb_hi),
                                             stop=(k == KT - 1 and part == 1))
                if k == KT - 1:
                    last.then_inc(projected, 1)
                elif isinstance(n, int) and n == NB - 1:
                    last.then_inc(wb_used, 1)

            def turn_qk(p, b):
                n = index(p, b)
                if isinstance(n, int) and n == 0:
                    pe.wait_ge(ident_in, 16)
                pe.wait_ge(q_copied, n + 1)
                for j in range(H // 2):
                    last = turn(bank[T_BANK][:, j * P:(j + 1) * P], q_tok[:, b, j * P:(j + 1) * P])
                last.then_inc(qk_turned, 1)
                pe.wait_ge(k_copied, n + 1)
                turn(bank[T_BANK + 1][:, 0:P], k_tok[:, b, :]).then_inc(qk_turned, 1)

            def first_block(p, b):
                n = index(p, b)
                return isinstance(n, int) and n == 0

            def score(p, b):
                n = index(p, b)
                keys = P if first_block(p, b) else 2 * P
                pe.wait_ge(stacked, n + 1)
                for h in range(H):
                    for part in range(2):
                        moving = k_stack[:, part * G + h // GH, :, :].rearrange("p s k -> p (s k)")
                        last = pe.matmul(bank[T_BANK + h // 2][:, (h % 2) * 2 * P:(h % 2) * 2 * P + keys],
                                         q_stack[:, h, :], moving[:, 0:keys],
                                         start=(part == 0), stop=(part == 1))
                    if h % 2 == 1:
                        last.then_inc(scored, 1)

            def turn_probs(p, b, half):
                n = index(p, b)
                for h in range(4 * half, 4 * half + 4):
                    pe.wait_ge(exp_set, 8 * n + h + 1)
                    last = turn(bank[T_BANK + half][:, (h % 4) * P:(h % 4 + 1) * P], probs[:, h, 0:P])
                last.then_inc(p_turned, 1)

            def attend(p, b):
                n = index(p, b)
                pe.wait_ge(v_set, n + 1)
                ge(pe, o_read, n)
                slots = range(1 if first_block(p, b) else 2)
                for h in range(H):
                    if h % 4 == 0:
                        pe.wait_ge(p_copied, 2 * n + 1 + h // 4)
                    g = h // GH
                    for s in slots:
                        last = pe.matmul(bank[O_BANK][:, h * HD:(h + 1) * HD], probs_t[:, h, s, :],
                                         v_tok[:, s, g * HD:(g + 1) * HD],
                                         start=(s == 0), stop=(s == slots[-1]))
                last.then_inc(attended, 1)

            def step(p, b):
                now, behind, last = (p, b), later(p, b, -1), later(p, b, -2)
                if exists(*last):
                    attend(*last)
                for k in range(KT):
                    project_k(*now, k)
                    if exists(*behind):
                        if k == 0:
                            turn_qk(*behind)
                        if k == 2:
                            score(*behind)
                        if k == 5:
                            turn_probs(*behind, 0)
                        if k == 6:
                            turn_probs(*behind, 1)

            pe.wait_ge(ones_set, 1)
            pe.wait_ge(rel_spread, H)
            for half in range(2):
                pe.matmul(bank[5 + half][:, :], ones, rel_rows[:, 4 * half:4 * half + 4, :].rearrange("b h j -> b (h j)"),
                          start=True, stop=True).then_inc(rel_summed, 1)
            run_b(pe, step)

            def project_a(p, b, tiles, first=False, last_tiles=False):
                n = index(p, b)
                if first:
                    pe.wait_ge(xa_lo_set, n + 1)
                if isinstance(n, int) and n == 0:
                    banks = ((0, q_copied, NB), (2, gate_b_set, NB), (1, v_set, NB))
                else:
                    banks = ((1, v_act_set, n), (2, z_read, n), (0, u_read, n))
                if len(tiles) > 1:
                    order = [(at, part, k) for at in banks for k in tiles for part in range(2)]
                else:
                    order = [(at, part, k) for k in tiles for part in range(2) for at in banks]
                for (j, emptied, count), part, k in order:
                    opens = first and part == 0 and k == tiles[0]
                    if opens:
                        pe.wait_ge(emptied, count)
                    for w in (wa_hi, wa_lo)[:2 - part]:
                        last = pe.matmul(bank[j][:, :], xt_of(n)[:, part, k, :], w[:, k, j * AW:(j + 1) * AW],
                                         start=(opens and w is wa_hi),
                                         stop=(last_tiles and part == 1 and k == tiles[-1]))
                if last_tiles:
                    last.then_inc(a_projected, 1)

            def turn_y(p, b, part):
                n = index(p, b)
                if part == 0:
                    ge(pe, yt_lo_set, 2 * n)
                    pe.wait_ge(ya_set, n + 1)
                else:
                    pe.wait_ge(yt_lo_set, 2 * n + 1)
                    pe.wait_ge(yb_loaded, 16 * n + 16)
                source = yb_in if part else gate_a[b]
                for k in range(4):
                    last = turn(bank[5][:, k * P:(k + 1) * P], source[:, k * P:(k + 1) * P])
                last.then_inc(y_turned, 1)

            def project_y(p, b, k):
                n = index(p, b)
                if k % 4 == 0:
                    pe.wait_ge(yt_lo_set, 2 * n + 1 + k // 4)
                if k == 0 and isinstance(n, int) and n == NB - 2:
                    pe.wait_ge(v_act_set, NB)
                    pe.wait_ge(u_read, NB)
                elif k == 0 and isinstance(n, int) and n == NB - 1:
                    pe.wait_ge(mix_read, NB)
                elif k == 0:
                    ge(pe, post_set, n)
                if isinstance(n, int) and n == 0:
                    pe.wait_ge(wo_lo_set, k + 1)
                for part in range(2):
                    for half in range(2):
                        for w in (wo_hi, wo_lo)[:2 - part]:
                            last = pe.matmul(bank[y_banks(n)[half]][:, :], yt_of(n)[:, part, k, :],
                                             w[:, k, half * HALF:(half + 1) * HALF],
                                             start=(k == 0 and part == 0 and w is wo_hi),
                                             stop=(k == KT - 1 and part == 1))
                if k == KT - 1:
                    last.then_inc(y_projected, 1)

            def mix(p):
                pe.wait_ge(vn_set, 2 * p + 2)
                ge(pe, mix_read, 2 * p)
                for g in range(AG):
                    at = (g % 4) * 2 * AD
                    last = pe.matmul(bank[6 + g // 4][:, at:at + 2 * AD], ws_t[:, g, :],
                                     act_buf[:, 0:2, g * AD:(g + 1) * AD], start=True, stop=True)
                last.then_inc(mixed, 1)

            def step_a(p, b):
                now, behind = (p, b), later(p, b, -2)
                for k in range(KT):
                    project_a(*now, (k,), first=(k == 0), last_tiles=(k == KT - 1))
                    if k == 1:
                        turn_y(*behind, 0)
                    if k == 3:
                        turn_y(*behind, 1)
                for k in range(KT):
                    project_y(*behind, k)
                    if k == 4 and b == 1:
                        mix(p)

            last_b, before_last = ((NB - 1) // 2, (NB - 1) % 2), ((NB - 2) // 2, (NB - 2) % 2)
            attend(*before_last)
            for i, k in enumerate(FIRST_USED):
                pe.wait_ge(wa_lo_set, i + 1)
                project_a(0, 0, (k,), first=(i == 0), last_tiles=(i == KT - 1))
                if i == 0:
                    turn_qk(*last_b)
                if i == 2:
                    score(*last_b)
            pe.wait_ge(ws_masked, 1)
            project_a(0, 1, range(3), first=True)
            turn_probs(*last_b, 0)
            project_a(0, 1, (3,))
            turn_probs(*last_b, 1)
            project_a(0, 1, (4,))
            attend(*last_b)
            for k in range(5, KT):
                project_a(0, 1, (k,), last_tiles=(k == KT - 1))
            project_a(1, 0, range(3), first=True)
            for k in range(3, KT):
                if k == 4:
                    pe.wait_ge(o_read, NB)
                    mix(0)
                if k == KT - 1:
                    turn_y(0, 0, 0)
                project_a(1, 0, (k,), last_tiles=(k == KT - 1))
            turn_y(0, 0, 1)
            for k in range(KT):
                project_y(0, 0, k)
            run_a(pe, step_a)
            last_pair = NB // 2 - 1
            turn_y(last_pair, 0, 0)
            turn_y(last_pair, 0, 1)
            for k in range(KT):
                project_y(last_pair, 0, k)
                if k == 1:
                    turn_y(last_pair, 1, 0)
                if k == 3:
                    turn_y(last_pair, 1, 1)
            for k in range(KT):
                project_y(last_pair, 1, k)

        @block.scalar
        def _(act):
            def copy(target, source, scale=1.0):
                return act.activation(target, source, ACTF.Copy, scale=scale)

            def turned_hi(p, b):
                n = index(p, b)
                act.wait_ge(xt_in[b], 16 * p + 16)
                copy(xt[:, b, 0], xt_raw[:, b, 1]).then_inc(xt_hi_set, 1)

            def square(p, b):
                n = index(p, b)
                act.wait_ge(x_in[b], 16 * p + 16)
                ge(act, x_squared, n)
                act.activation(squares, xs[:, b, :], ACTF.Square, scale=float(D) ** -0.5,
                               accum_out=mean_sq_x(b)).then_inc(x_squared, 1)

            def leave_projection(p, b):
                n = index(p, b)
                act.wait_ge(rstd_set, n + 1)
                act.wait_ge(projected, n + 1)
                copy(q_tok[:, b, :], bank[Q_BANK][:, :], rstd_b(b, 1)).then_inc(q_copied, 1)
                copy(k_tok[:, b, :], bank[KV_BANK][:, 0:KVW], rstd_b(b, 0)).then_inc(k_copied, 1)
                ge(act, yb_set, n - 1)
                act.activation(gate_b[:, b, :], bank[Z_BANK][:, :], ACTF.Tanh, scale=rstd_b(b, 2)).then_inc(z_tanh_set, 1)
                ge(act, attended, n)
                copy(v_tok[:, b, :], bank[KV_BANK][:, KVW:2 * KVW], rstd_b(b, 0)).then_inc(v_set, 1)

            def stack_hi(p, b):
                n = index(p, b)
                act.wait_ge(qk_turned, 2 * n + 1)
                for j in range(2):
                    rows = slice(HD * j, HD * j + HD)
                    copy(q_stack[rows, j::2, :], bank[T_BANK][rows, :].rearrange("p (h t) -> p h t", t=P)).then_inc(stack_hi_set, 1)
                act.wait_ge(qk_turned, 2 * n + 2)
                for g in range(G):
                    rows = slice(HD * g, HD * g + HD)
                    for c in (g, 1 - g):
                        last = copy(k_stack[HD * c:HD * c + HD, g, b, :], bank[T_BANK + 1][rows, 0:P])
                    last.then_inc(stack_hi_set, 1)

            def exponentials(p, b, half):
                n = index(p, b)
                for h in range(4 * half, 4 * half + 4):
                    if h % 4 == 0:
                        act.wait_ge(max_set, 2 * n + 1 + h // 4)
                    act.activation(probs[:, h, 0:P], probs[:, h, 0:P], ACTF.Exp,
                                   bias=neg_max[:, h:h + 1], accum_out=row_sum[:, h:h + 1]).then_inc(exp_set, 1)
                if half == 1:
                    act.activation(sink_exp, sink_diff, ACTF.Exp).then_inc(sink_exp_set, 1)

            def split_a(i):
                k = FIRST_USED[i]
                act.wait_ge(wa_in[k], 16)
                wait_wb_used(act, hi_after(k))
                source = wa_stage if k in STAGED else wa_raw
                copy(wa_hi[:, k, :], source[:, k, :], gain[:, k:k + 1]).then_inc(wa_hi_set, 1)

            def step(p, b):
                ahead, behind = later(p, b, 1), later(p, b, -1)
                if not exists(*behind):
                    square(*ahead)
                    return
                leave_projection(*behind)
                if exists(*ahead):
                    turned_hi(*ahead)
                    stack_hi(*behind)
                    square(*ahead)
                else:
                    turned_hi_a(0, 0)
                    stack_hi(*behind)
                    for i in range(2):
                        split_a(i)
                exponentials(*behind, 0)
                exponentials(*behind, 1)
                if not exists(*ahead):
                    split_a(2)

            def turned_hi_a(p, b):
                n = index(p, b)
                act.wait_ge(xta_in, 16 * n + 16)
                copy(xt_of(n)[:, 0], xt_raw[:, 1 if isinstance(n, int) and n == 1 else 0, 1]).then_inc(xa_hi_set, 1)

            act.wait_ge(gain_in, 16)
            turned_hi(0, 0)
            for k in range(KT):
                if k == KT - 2:
                    square(0, 0)
                if k == KT - 1:
                    turned_hi(0, 1)
                act.wait_ge(wb_in[k], 16)
                copy(wb_hi[:, k, :], wb_raw[:, k, :], gain[:, k:k + 1]).then_inc(wb_hi_set, 1)
            run_b(act, step)

            def leave_projection_a(p, b):
                n = index(p, b)
                act.wait_ge(rstd_a_set, n + 1)
                act.wait_ge(a_projected, n + 1)
                if not isinstance(n, int) or n >= 2:
                    act.wait_ge(ya_set, n - 1)
                    act.wait_ge(y_turned, 2 * (n - 1) - 1)
                act.activation(v_act[b], bank[1][:, :], ACTF.Gelu_apprx_tanh, scale=rstd_a(b, 0)).then_inc(v_act_set, 1)
                act.activation(gate_a[b], bank[2][:, :], ACTF.Tanh, scale=rstd_a(b, 1)).then_inc(za_tanh_set, 1)
                act.activation(bank[0][:, :], bank[0][:, :], ACTF.Gelu_apprx_tanh, scale=rstd_a(b, 0)).then_inc(u_act_set, 1)

            def ready_gelu(j):
                act.activation(small[:, 22 + j:23 + j], gain[:, 0:1], ACTF.Gelu_apprx_tanh)

            def turned_hi_y(p, b):
                n = index(p, b)
                for half in range(2):
                    act.wait_ge(y_turned, 2 * n + 1 + half)
                    if half == 0 and isinstance(n, int) and n == NB - 2:
                        act.wait_ge(a_projected, NB)
                    elif half == 0:
                        ge(act, y_projected, n - 1 if isinstance(n, int) and n == NB - 1 else n)
                    copy(yt_of(n)[:, 0, 4 * half:4 * half + 4, :],
                         bank[5][:, :].rearrange("p (k t) -> p k t", k=4)).then_inc(yt_hi_set, 1)

            def step_a(p, b):
                ahead, behind = later(p, b, 1), later(p, b, -2)
                turned_hi_y(*behind)
                leave_projection_a(p, b)
                if exists(*ahead):
                    turned_hi_a(*ahead)

            last_b = ((NB - 1) // 2, (NB - 1) % 2)
            leave_projection(*last_b)
            split_a(3)
            stack_hi(*last_b)
            for i in range(4, KT):
                split_a(i)
            turned_hi_a(0, 1)
            ready_gelu(0)
            leave_projection_a(0, 0)
            exponentials(*last_b, 0)
            exponentials(*last_b, 1)
            for k in range(KT):
                if k == 0:
                    act.wait_ge(p_turned, 2 * NB)
                if k == 2:
                    turned_hi_a(1, 0)
                    act.wait_ge(attended, NB)
                if k == 5:
                    ready_gelu(1)
                    leave_projection_a(0, 1)
                    for j in range(2):
                        act.wait_ge(yb_stored[j], 16 * (NB // 2))
                act.wait_ge(wo_in[k], 16)
                copy(wo_hi[:, k, :], wo_raw[:, k, :]).then_inc(wo_hi_set, 1)
            step_a(1, 0)
            run_a(act, step_a)
            turned_hi_y(NB // 2 - 1, 0)
            turned_hi_y(NB // 2 - 1, 1)

        @block.vector
        def _(dve):
            def turned_lo(p, b):
                n = index(p, b)
                dve.wait_ge(xt_hi_set, n + 1)
                dve.tensor_tensor(xt[:, b, 1], xt_raw[:, b, 1], xt[:, b, 0].bitcast(F32), ALU.subtract).then_inc(xt_lo_set, 1)

            STEPS_X = 1 + RSQRT_STEPS

            def rms_of_x(p, b):
                n = index(p, b)
                base = STEPS_X * n
                dve.wait_ge(x_squared, n + 1)
                dve.tensor_scalar(mean_sq, mean_sq_x(b), NORM_EPS, None, ALU.add).then_inc(stats_steps, 1)
                dve.wait_ge(stats_steps, base + 1)
                rsqrt(dve, stats_steps, base + 1, mean_sq, rstd_b(b, 0), newton)
                dve.tensor_scalar(rstd_b(b, 1), rstd_b(b, 0), float(HD) ** -0.5, None, ALU.mult)
                dve.tensor_scalar(rstd_b(b, 2), rstd_b(b, 0), 0.5, None, ALU.mult)
                column = rstd_all[:, n:n + 1] if isinstance(n, int) else rstd_all[:, bass.ds(n, 1)]
                dve.tensor_copy(column, rstd_b(b, 0)).then_inc(rstd_set, 1)

            def leave_projection(p, b):
                n = index(p, b)
                dve.wait_ge(z_tanh_set, n + 1)
                dve.tensor_scalar(gate_b[:, b, :], gate_b[:, b, :], 1.0, rstd_b(b, 2), ALU.add, ALU.mult).then_inc(gate_steps, 1)
                dve.wait_ge(gate_steps, n + 1)
                dve.tensor_tensor(gate_b[:, b, :], bank[Z_BANK][:, :], gate_b[:, b, :], ALU.mult).then_inc(gate_b_set, 1)

            def stack_lo(p, b):
                n = index(p, b)
                for j in range(2):
                    rows, other = slice(HD * j, HD * j + HD), slice(HD * (1 - j), HD * (1 - j) + HD)
                    dve.wait_ge(stack_hi_set, 4 * n + 1 + j)
                    dve.tensor_tensor(q_stack[other, j::2, :], bank[T_BANK][rows, :].rearrange("p (h t) -> p h t", t=P),
                                      q_stack[rows, j::2, :].bitcast(F32), ALU.subtract)
                for g in range(G):
                    rows = slice(HD * g, HD * g + HD)
                    dve.wait_ge(stack_hi_set, 4 * n + 3 + g)
                    for c in (g, 1 - g):
                        last = dve.tensor_tensor(k_stack[HD * c:HD * c + HD, G + g, b, :], bank[T_BANK + 1][rows, 0:P],
                                                 k_stack[rows, g, b, :].bitcast(F32), ALU.subtract)
                last.then_inc(stacked, 1)

            STEPS_S = 7

            def soft_max(p, b, between_halves=None):
                n = index(p, b)
                first = isinstance(n, int) and n == 0
                base = 0 if first else STEPS_S * n - 2
                keys = P if isinstance(n, int) and n == 0 else 2 * P
                at = P if b == 0 else 0
                if isinstance(n, int) and n == 0:
                    dve.wait_ge(bias_in, 16 * 2)
                    dve.wait_ge(own_keys_set, 2)
                for half in range(2):
                    part = slice(4 * half, 4 * half + 4)
                    for j in range(2 * half, 2 * half + 2):
                        dve.wait_ge(scored, 4 * n + j + 1)
                        last = dve.tensor_tensor(probs[:, 2 * j:2 * j + 2, 0:keys],
                                                 bank[T_BANK + j][:, :].rearrange("p (h k) -> p h k", h=2)[:, :, 0:keys],
                                                 bias[:, 2 * j:2 * j + 2, at:at + keys], ALU.add)
                    last.then_inc(softmax_steps, 1)
                    base += 1
                    dve.wait_ge(softmax_steps, base)
                    if not first:
                        dve.tensor_tensor(probs[:, part, 0:P], probs[:, part, 0:P], probs[:, part, P:2 * P], ALU.max).then_inc(softmax_steps, 1)
                        base += 1
                        dve.wait_ge(softmax_steps, base)
                    dve.tensor_reduce(row_max[:, part], probs[:, part, 0:P], mybir.AxisListType.X, ALU.max).then_inc(softmax_steps, 1)
                    base += 1
                    dve.wait_ge(softmax_steps, base)
                    negated = dve.scalar_tensor_tensor(out=neg_max[:, part], in0=row_max[:, part], scalar=-1.0,
                                                       in1=neg_sink[:, part], op0=ALU.mult, op1=ALU.min)
                    negated.then_inc(softmax_steps if half else max_set, 1)
                    if half == 0 and between_halves:
                        between_halves()
                dve.wait_ge(softmax_steps, base + 1)
                dve.tensor_tensor(sink_diff, neg_max, neg_sink[:, :], ALU.subtract).then_inc(max_set, 1)

            def leave_probs(p, b, half):
                n = index(p, b)
                heads = slice(4 * half, 4 * half + 4)
                turned = bank[T_BANK + half][:, :].rearrange("p (h t) -> p h t", h=4)
                dve.wait_ge(p_turned, 2 * n + 1 + half)
                own = dve.tensor_tensor(probs_t[:, heads, b, :], turned, own_keys[:, :].unsqueeze(1).to_broadcast([P, 4, P]), ALU.mult)
                if isinstance(n, int) and n == 0:
                    own.then_inc(p_copied, 1)
                    return
                own.then_inc(p_parted, 1)
                dve.wait_ge(p_parted, 2 * (n - 1) + 1 + half)
                dve.tensor_tensor(probs_t[:, heads, 1 - b, :], turned, probs_t[:, heads, b, :], ALU.subtract).then_inc(p_copied, 1)

            def denominators(p, b):
                n = index(p, b)
                dve.wait_ge(sink_exp_set, n + 1)
                dve.tensor_tensor(row_sum, row_sum, sink_exp, ALU.add).then_inc(denominator_steps, 1)
                dve.wait_ge(denominator_steps, 2 * n + 1)
                dve.reciprocal(row_inv, row_sum).then_inc(denominator_steps, 1)
                dve.wait_ge(denominator_steps, 2 * n + 2)

            def gate(p, b):
                n = index(p, b)
                dve.wait_ge(attended, n + 1)
                ge(dve, yb_stored[b], 16 * p)
                dve.tensor_tensor(y_b[:, b, :].rearrange("p (h d) -> p h d", h=H),
                                  bank[O_BANK][:, :].rearrange("p (h d) -> p h d", h=H),
                                  row_inv.unsqueeze(2).to_broadcast([P, H, HD]), ALU.mult).then_inc(o_read, 1)
                dve.wait_ge(o_read, n + 1)
                dve.tensor_tensor(y_b[:, b, :], y_b[:, b, :], gate_b[:, b, :], ALU.mult).then_inc(yb_set, 1)

            def split_a(i):
                k = FIRST_USED[i]
                dve.wait_ge(wa_hi_set, i + 1)
                wait_wb_used(dve, lo_after(k))
                source = wa_stage if k in STAGED else wa_raw
                dve.scalar_tensor_tensor(out=wa_lo[:, k, :], in0=source[:, k, :], scalar=gain[:, k:k + 1],
                                         in1=wa_hi[:, k, :].bitcast(F32), op0=ALU.mult, op1=ALU.subtract).then_inc(wa_lo_set, 1)

            def turned_lo_a(p, b):
                n = index(p, b)
                dve.wait_ge(xa_hi_set, n + 1)
                raw = xt_raw[:, 1 if isinstance(n, int) and n == 1 else 0, 1]
                dve.tensor_tensor(xt_of(n)[:, 1], raw, xt_of(n)[:, 0].bitcast(F32), ALU.subtract).then_inc(xa_lo_set, 1)

            def step(p, b):
                ahead, behind, last = later(p, b, 1), later(p, b, -1), later(p, b, -2)
                if not exists(*behind):
                    return
                leave_projection(*behind)
                if exists(*last):
                    gate(*last)
                else:
                    rms_of_x(p, b)
                stack_lo(*behind)
                if exists(*ahead):
                    turned_lo(*ahead)
                    soft_max(*behind)
                    rms_of_x(*ahead)
                else:
                    turned_lo_a(0, 0)
                    soft_max(*behind)
                    split_a(0)
                leave_probs(*behind, 0)
                leave_probs(*behind, 1)
                denominators(*behind)

            dve.wait_ge(buckets_in, 16 * 2)
            for h in range(H):
                dve.tensor_scalar(rel_rows[:, h, :], onehot, rel[:, h:h + 1], None, ALU.mult).then_inc(rel_spread, 1)
            turned_lo(0, 0)
            dve.wait_ge(rel_summed, 2)
            dve.wait_ge(rows_set, 1)
            dve.tensor_copy(bias_rows[:, 0:4, P:2 * P], bank[5][:, :].rearrange("p (h j) -> p h j", h=4))
            dve.tensor_copy(bias_rows[:, 4:8, P:2 * P], bank[6][:, :].rearrange("p (h j) -> p h j", h=4)).then_inc(rows_set, 1)
            dve.wait_ge(gain_in, 16)
            for k in range(KT):
                if k == KT - 2:
                    rms_of_x(0, 0)
                if k == KT - 1:
                    turned_lo(0, 1)
                dve.wait_ge(wb_hi_set, k + 1)
                dve.scalar_tensor_tensor(out=wb_lo[:, k, :], in0=wb_raw[:, k, :], scalar=gain[:, k:k + 1],
                                         in1=wb_hi[:, k, :].bitcast(F32), op0=ALU.mult, op1=ALU.subtract).then_inc(wb_lo_set, 1)
            dve.wait_ge(sinks_in, 16)
            dve.tensor_scalar(neg_sink[:, :], neg_sink[:, :], -1.0, None, ALU.mult).then_inc(sink_negated, 1)
            dve.wait_ge(sink_negated, 1)
            run_b(dve, step)

            def rstd_of_pass_b(p, b):
                n = index(p, b)
                column = rstd_all[:, n:n + 1] if isinstance(n, int) else rstd_all[:, bass.ds(n, 1)]
                dve.tensor_copy(rstd_a(b, 0), column).then_inc(rstd_a_steps, 1)
                dve.wait_ge(rstd_a_steps, n + 1)
                dve.tensor_scalar(rstd_a(b, 1), rstd_a(b, 0), 0.5, None, ALU.mult).then_inc(rstd_a_set, 1)

            STEPS_LN = 5 + RSQRT_STEPS

            def layer_norm(p, b):
                n = index(p, b)
                base = STEPS_LN * n
                done = 0

                def link(ins, then_aggregate=False):
                    nonlocal done
                    done += 1
                    ins.then_inc(ln_steps, 1)
                    dve.wait_ge(ln_steps, base + done)
                    if then_aggregate:
                        dve.memset(newton, 0.0)

                v = v_act[b]
                dve.wait_ge(v_act_set, n + 1)
                link(dve.bn_stats(stats[:, 0, :], v), then_aggregate=True)
                link(dve.bn_aggr(mean_var, stats[:, 0:1, :]))
                link(dve.tensor_scalar(mean_sq, mean_var[:, 1:2], NORM_EPS, None, ALU.add))
                rsqrt(dve, ln_steps, base + done, mean_sq, rstd_ln, newton)
                done += RSQRT_STEPS
                link(dve.tensor_scalar(v, v, mean_var[:, 0:1], rstd_ln, ALU.subtract, ALU.mult))
                link(dve.tensor_tensor(v, v, ln_gain[:, :], ALU.mult))
                dve.tensor_tensor(v, v, ln_bias[:, :], ALU.add).then_inc(vn_set, 1)
                assert done == STEPS_LN

            def gate_of_a(p, b):
                n = index(p, b)
                dve.wait_ge(za_tanh_set, n + 1)
                dve.tensor_scalar(gate_a[b], gate_a[b], 1.0, rstd_a(b, 1), ALU.add, ALU.mult).then_inc(gate_a_steps, 1)
                dve.wait_ge(gate_a_steps, n + 1)
                dve.tensor_tensor(gate_a[b], bank[2][:, :], gate_a[b], ALU.mult).then_inc(z_read, 1)
                dve.wait_ge(z_read, n + 1)
                dve.wait_ge(u_act_set, n + 1)
                dve.tensor_tensor(gate_a[b], bank[0][:, :], gate_a[b], ALU.mult).then_inc(u_read, 1)

            def gate_mixed(p):
                dve.wait_ge(mixed, p + 1)
                for b in range(2):
                    for half in range(2):
                        groups = slice(4 * half, 4 * half + 4)
                        last = dve.tensor_tensor(
                            v_act[b].rearrange("p (g d) -> p g d", g=AG)[:, groups, :],
                            bank[6 + half][:, :].rearrange("p (g c d) -> p g c d", g=4, c=2)[:, :, b, :],
                            bs_t[:, groups].unsqueeze(2).to_broadcast([P, 4, AD]), ALU.add)
                    last.then_inc(mix_read, 1)
                for b in range(2):
                    dve.wait_ge(mix_read, 2 * p + b + 1)
                    dve.wait_ge(u_read, 2 * p + b + 1)
                    dve.tensor_tensor(gate_a[b], gate_a[b], v_act[b], ALU.mult).then_inc(ya_set, 1)

            def turned_lo_y(p, b):
                n = index(p, b)
                for half in range(2):
                    dve.wait_ge(yt_hi_set, 2 * n + 1 + half)
                    dve.tensor_tensor(yt_of(n)[:, 1, 4 * half:4 * half + 4, :],
                                      bank[5][:, :].rearrange("p (k t) -> p k t", k=4),
                                      yt_of(n)[:, 0, 4 * half:4 * half + 4, :].bitcast(F32), ALU.subtract).then_inc(yt_lo_set, 1)

            STEPS_POST = 7 + RSQRT_STEPS

            def post_norm(p, b):
                n = index(p, b)
                base = STEPS_POST * n
                done = 0

                def link(ins, then_aggregate=False):
                    nonlocal done
                    done += 1
                    ins.then_inc(post_steps, 1)
                    dve.wait_ge(post_steps, base + done)
                    if then_aggregate:
                        dve.memset(newton, 0.0)

                dve.wait_ge(xa_in[b], 16 * p + 16)
                dve.wait_ge(y_projected, n + 1)
                y = [bank[j] for j in y_banks(n)]
                dve.bn_stats(stats[:, 0, :], y[0][:, :])
                link(dve.bn_stats(stats[:, 1, :], y[1][:, :]), then_aggregate=True)
                link(dve.bn_aggr(mean_var, stats[:, :, :]))
                link(dve.scalar_tensor_tensor(out=mean_sq, in0=mean_var[:, 0:1], scalar=mean_var[:, 0:1],
                                              in1=mean_var[:, 1:2], op0=ALU.mult, op1=ALU.add))
                link(dve.tensor_scalar(mean_sq, mean_sq, NORM_EPS, None, ALU.add))
                rsqrt(dve, post_steps, base + done, mean_sq, rstd_post, newton)
                done += RSQRT_STEPS
                for half in range(2):
                    part = slice(half * HALF, (half + 1) * HALF)
                    link(dve.scalar_tensor_tensor(out=y[half][:, :], in0=y[half][:, :], scalar=rstd_post,
                                                  in1=post_gain[:, part], op0=ALU.mult, op1=ALU.mult))
                    last = dve.tensor_tensor(xs[:, b, part], xs[:, b, part], y[half][:, :], ALU.add)
                    if half == 0:
                        link(last)
                last.then_inc(post_set, 1)
                assert done == STEPS_POST

            def step_a(p, b):
                ahead, behind = later(p, b, 1), later(p, b, -2)
                turned_lo_y(*behind)
                layer_norm(p, b)
                gate_of_a(p, b)
                if exists(*ahead):
                    turned_lo_a(*ahead)
                    rstd_of_pass_b(*ahead)
                if b == 1:
                    gate_mixed(p)
                if not exists(*ahead):
                    turned_lo_y(NB // 2 - 1, 0)
                    turned_lo_y(NB // 2 - 1, 1)
                post_norm(*behind)

            def split_o(k):
                dve.wait_ge(wo_hi_set, k + 1)
                dve.tensor_tensor(wo_lo[:, k, :], wo_raw[:, k, :], wo_hi[:, k, :].bitcast(F32), ALU.subtract).then_inc(wo_lo_set, 1)

            last_b, before_last = ((NB - 1) // 2, (NB - 1) % 2), ((NB - 2) // 2, (NB - 2) % 2)
            rstd_of_pass_b(0, 0)
            leave_projection(*last_b)
            split_a(1)
            split_a(2)
            gate(*before_last)
            stack_lo(*last_b)
            for i in range(3, KT):
                split_a(i)
            turned_lo_a(0, 1)
            soft_max(*last_b, between_halves=lambda: gate_of_a(0, 0))
            rstd_of_pass_b(0, 1)
            leave_probs(*last_b, 0)
            leave_probs(*last_b, 1)
            denominators(*last_b)
            dve.wait_ge(consts_in, 16 * 4)
            layer_norm(0, 0)
            turned_lo_a(1, 0)
            rstd_of_pass_b(1, 0)
            gate(*last_b)
            for k in range(2):
                split_o(k)
            gate_of_a(0, 1)
            layer_norm(0, 1)
            for k in range(2, 5):
                split_o(k)
            gate_mixed(0)
            for k in range(5, KT):
                split_o(k)
            step_a(1, 0)
            run_a(dve, step_a)
            post_norm(NB // 2 - 1, 0)
            post_norm(NB // 2 - 1, 1)


def kernel(x, pre_norm_g, w_in, ln_v_g, ln_v_b, w_spatial, b_spatial, sinks, rel_bias, w_out, post_norm_g):
    import concourse.bacc as bacc
    from concourse.bass_utils import run_bass_kernel_spmd

    buckets = rel_bias.shape[0]
    distance = np.arange(P - 1, -1, -1)
    exact = buckets // 2
    far = exact + (np.log(np.maximum(distance, 1) / exact) / math.log(REL_MAX_DIST / exact) * (buckets - exact)).astype(np.int32)
    bucket = np.where(distance < exact, distance, np.minimum(far, buckets - 1))
    onehot = np.equal(np.arange(buckets)[:, None], bucket[None, :]).astype(np.float32)

    arrays = {
        "x": x, "x_turned": x[0].reshape(-1, P, x.shape[2] // P, P).transpose(0, 3, 2, 1), "pre_norm_g": pre_norm_g.reshape(-1, P).T, "w_in": w_in, "ln_v_g": ln_v_g, "ln_v_b": ln_v_b,
        "w_spatial": w_spatial[0].transpose(2, 0, 1), "b_spatial": b_spatial[0].T, "sinks": sinks, "rel_bias": rel_bias,
        "w_out": w_out, "post_norm_g": post_norm_g, "bucket_onehot": onehot, "identity": np.eye(P, dtype=np.float32),
    }
    arrays = {f"in_{name}": np.ascontiguousarray(a) for name, a in arrays.items()}
    nc = bacc.Bacc("TRN2", target_bir_lowering=False, num_devices=1)
    args = [nc.dram_tensor(name, a.shape, mybir.dt.from_np(a.dtype), kind="ExternalInput").ap() for name, a in arrays.items()]
    out = nc.dram_tensor("out", x.shape, F32, kind="ExternalOutput").ap()
    build(nc, *args, out)
    result = run_bass_kernel_spmd(nc, [arrays], core_ids=[0])
    return result.results[0]["out"]
```
